# Optimizing a Trainium2 kernel written in Bass

```python
import jax, jax.numpy as jnp
from jax import lax
import numpy as np

D_MODEL = 1024
BATCH = 1
SEQ = 256
DEPTH = 2
DEC_BATCH = 8
DEC_SEQ = 4
PAST_LEN = 2048
PAGE_SIZE = 128

N_MIXERS = 2
N_A_LAYERS = (DEPTH + 1) // 2
N_B_LAYERS = DEPTH // 2
D_RNN = D_MODEL
N_RG_BLOCKS = 16
RG_BLOCK = D_RNN // N_RG_BLOCKS
RG_CONV_W = 4
RG_C = 8.0
D_CONV = D_MODEL
CONF_CONV_W = 31
N_KEYS = 128
N_EXPERTS = N_KEYS * N_KEYS
N_RHEADS = 8
D_KEY = 256
D_HALF = D_KEY // 2
TOPK = 16
EXPERT_BLOCK = 128
EPS = 1e-6

kernel_name = 'hawk_conformer_peer_hybrid_step'

def rmsnorm(x, g):
    xf = x.astype(jnp.float32)
    y = xf * lax.rsqrt(jnp.mean(xf * xf, axis=-1, keepdims=True) + EPS)
    return (y * g.astype(jnp.float32)).astype(x.dtype)

def layernorm(x, g, b):
    xf = x.astype(jnp.float32)
    mu = jnp.mean(xf, axis=-1, keepdims=True)
    xc = xf - mu
    var = jnp.mean(xc * xc, axis=-1, keepdims=True)
    y = xc * lax.rsqrt(var + EPS) * g.astype(jnp.float32) + b.astype(jnp.float32)
    return y.astype(x.dtype)

def causal_depthwise(x_ext, w, b):
    c = x_ext.shape[-1]
    y = lax.conv_general_dilated(
        x_ext, w[:, None, :].astype(x_ext.dtype), window_strides=(1,), padding='VALID',
        dimension_numbers=('NWC', 'WIO', 'NWC'), feature_group_count=c)
    return y + b.astype(x_ext.dtype)

def rg_lru(x, h0, w_a, b_a, w_i, b_i, lam):
    nb, t, _ = x.shape
    xf = x.astype(jnp.float32)
    xb = xf.reshape(nb, t, N_RG_BLOCKS, RG_BLOCK)
    r = jax.nn.sigmoid(jnp.einsum('btni,nij->btnj', xb, w_a.astype(jnp.float32)).reshape(nb, t, D_RNN)
                       + b_a.astype(jnp.float32))
    i = jax.nn.sigmoid(jnp.einsum('btni,nij->btnj', xb, w_i.astype(jnp.float32)).reshape(nb, t, D_RNN)
                       + b_i.astype(jnp.float32))
    log_a = -RG_C * r * jax.nn.softplus(-lam.astype(jnp.float32))
    a = jnp.exp(log_a)
    u = jnp.sqrt(-jnp.expm1(2.0 * log_a)) * (i * xf)
    u = u.at[:, 0].add(a[:, 0] * h0.astype(jnp.float32))

    def combine(c1, c2):
        a1, b1 = c1
        a2, b2 = c2
        return a1 * a2, a2 * b1 + b2

    _, h = lax.associative_scan(combine, (a, u), axis=1)
    return h

def recurrent_mixer(xn, h0, conv_buf, w_in, conv_w, conv_b, w_a, b_a, w_i, b_i, lam, w_out):
    proj = xn @ w_in
    gate = jax.nn.gelu(proj[..., :D_RNN])
    xr = proj[..., D_RNN:]
    x_ext = jnp.concatenate([conv_buf.astype(xr.dtype), xr], axis=1)
    xc = causal_depthwise(x_ext, conv_w, conv_b)
    h = rg_lru(xc, h0, w_a, b_a, w_i, b_i, lam)
    y = (h.astype(xn.dtype) * gate) @ w_out
    return y, h[:, -1].astype(xn.dtype), x_ext[:, -(RG_CONV_W - 1):]

def conformer_mixer(xn, conv_buf, w_pw1, b_pw1, dw_w, dw_b, ln_g, ln_b, w_pw2, b_pw2):
    p = xn @ w_pw1 + b_pw1
    z = p[..., :D_CONV] * jax.nn.sigmoid(p[..., D_CONV:])
    z_ext = jnp.concatenate([conv_buf.astype(z.dtype), z], axis=1)
    c = causal_depthwise(z_ext, dw_w, dw_b)
    c = jax.nn.silu(layernorm(c, ln_g, ln_b))
    y = c @ w_pw2 + b_pw2
    return y, z_ext[:, -(CONF_CONV_W - 1):]

def peer(xn, w_q, sub_keys, u_tab, v_tab):
    nb, t, d = xn.shape
    xt = xn.reshape(nb * t, d)
    n_tok = xt.shape[0]
    q = (xt @ w_q).astype(jnp.float32).reshape(n_tok, N_RHEADS, 2, D_HALF)
    s = jnp.einsum('thpc,hpkc->thpk', q, sub_keys.astype(jnp.float32))
    sv, si = lax.top_k(s, TOPK)
    cand = (sv[:, :, 0, :, None] + sv[:, :, 1, None, :]).reshape(n_tok, N_RHEADS, TOPK * TOPK)
    cand_idx = (si[:, :, 0, :, None] * N_KEYS + si[:, :, 1, None, :]).reshape(n_tok, N_RHEADS, TOPK * TOPK)
    best, pos = lax.top_k(cand, TOPK)
    eidx = jnp.take_along_axis(cand_idx, pos, axis=-1).reshape(n_tok, N_RHEADS * TOPK)
    g = jax.nn.softmax(best, axis=-1).reshape(n_tok, N_RHEADS * TOPK)
    n_pad = (-n_tok) % EXPERT_BLOCK
    n_blk = (n_tok + n_pad) // EXPERT_BLOCK
    xb = jnp.pad(xt, ((0, n_pad), (0, 0))).reshape(n_blk, EXPERT_BLOCK, d)
    ib = jnp.pad(eidx, ((0, n_pad), (0, 0))).reshape(n_blk, EXPERT_BLOCK, N_RHEADS * TOPK)
    gb = jnp.pad(g, ((0, n_pad), (0, 0))).reshape(n_blk, EXPERT_BLOCK, N_RHEADS * TOPK)

    def expert_block(args):
        xblk, iblk, gblk = args
        u = jnp.take(u_tab, iblk, axis=0)
        act = jax.nn.gelu(jnp.einsum('ted,td->te', u, xblk).astype(jnp.float32))
        w = (gblk * act).astype(xblk.dtype)
        v = jnp.take(v_tab, iblk, axis=0)
        return jnp.einsum('te,ted->td', w, v)

    out = lax.map(expert_block, (xb, ib, gb)).reshape(n_blk * EXPERT_BLOCK, d)[:n_tok]
    return out.reshape(nb, t, d)

def trunk(x, rg_h0, rg_conv0, cf_conv0, p):
    new_h, new_rgc, new_cfc = [], [], []
    for i in range(DEPTH):
        xn = rmsnorm(x, p['norm_mix'][i])
        j = i // N_MIXERS
        if i % N_MIXERS == 0:
            y, h_last, buf = recurrent_mixer(
                xn, rg_h0[j], rg_conv0[j], p['rg_w_in'][j], p['rg_conv_w'][j], p['rg_conv_b'][j],
                p['rg_w_a'][j], p['rg_b_a'][j], p['rg_w_i'][j], p['rg_b_i'][j], p['rg_lambda'][j],
                p['rg_w_out'][j])
            new_h.append(h_last)
            new_rgc.append(buf)
        else:
            y, buf = conformer_mixer(
                xn, cf_conv0[j], p['cf_w_pw1'][j], p['cf_b_pw1'][j], p['cf_dw_w'][j], p['cf_dw_b'][j],
                p['cf_ln_g'][j], p['cf_ln_b'][j], p['cf_w_pw2'][j], p['cf_b_pw2'][j])
            new_cfc.append(buf)
        x = x + y
        x = x + peer(rmsnorm(x, p['norm_ffn'][i]), p['peer_w_q'][i], p['peer_sub_keys'][i],
                     p['peer_u'][i], p['peer_v'][i])
    return rmsnorm(x, p['norm_final']), jnp.stack(new_h), jnp.stack(new_rgc), jnp.stack(new_cfc)

def setup_inputs(seed: int = 0) -> dict:
    key = jax.random.key(seed)
    ks = iter(jax.random.split(key, 40))
    f32 = jnp.float32

    def nrm(shape, scale):
        return jax.random.normal(next(ks), shape, f32) * scale

    x_prompt = nrm((BATCH, SEQ, D_MODEL), 1.0)
    x_sample = nrm((DEC_BATCH, DEC_SEQ, D_MODEL), 1.0)
    state_rglru_h = nrm((N_A_LAYERS, DEC_BATCH, D_RNN), 0.5)
    state_rglru_conv = nrm((N_A_LAYERS, DEC_BATCH, RG_CONV_W - 1, D_RNN), 1.0)
    state_conformer_conv = nrm((N_B_LAYERS, DEC_BATCH, CONF_CONV_W - 1, D_CONV), 0.5)
    norm_mix = 1.0 + nrm((DEPTH, D_MODEL), 0.02)
    norm_ffn = 1.0 + nrm((DEPTH, D_MODEL), 0.02)
    norm_final = 1.0 + nrm((D_MODEL,), 0.02)
    rg_w_in = nrm((N_A_LAYERS, D_MODEL, 2 * D_RNN), D_MODEL ** -0.5)
    rg_conv_w = nrm((N_A_LAYERS, RG_CONV_W, D_RNN), RG_CONV_W ** -0.5)
    rg_conv_b = nrm((N_A_LAYERS, D_RNN), 0.01)
    rg_w_a = nrm((N_A_LAYERS, N_RG_BLOCKS, RG_BLOCK, RG_BLOCK), RG_BLOCK ** -0.5)
    rg_b_a = nrm((N_A_LAYERS, D_RNN), 0.01)
    rg_w_i = nrm((N_A_LAYERS, N_RG_BLOCKS, RG_BLOCK, RG_BLOCK), RG_BLOCK ** -0.5)
    rg_b_i = nrm((N_A_LAYERS, D_RNN), 0.01)
    a_target = jax.random.uniform(next(ks), (N_A_LAYERS, D_RNN), f32, 0.9, 0.999)
    p_sig = a_target ** (1.0 / RG_C)
    rg_lambda = jnp.log(p_sig) - jnp.log1p(-p_sig)
    rg_w_out = nrm((N_A_LAYERS, D_RNN, D_MODEL), D_RNN ** -0.5)
    cf_w_pw1 = nrm((N_B_LAYERS, D_MODEL, 2 * D_CONV), D_MODEL ** -0.5)
    cf_b_pw1 = nrm((N_B_LAYERS, 2 * D_CONV), 0.01)
    cf_dw_w = nrm((N_B_LAYERS, CONF_CONV_W, D_CONV), CONF_CONV_W ** -0.5)
    cf_dw_b = nrm((N_B_LAYERS, D_CONV), 0.01)
    cf_ln_g = 1.0 + nrm((N_B_LAYERS, D_CONV), 0.02)
    cf_ln_b = nrm((N_B_LAYERS, D_CONV), 0.01)
    cf_w_pw2 = nrm((N_B_LAYERS, D_CONV, D_MODEL), D_CONV ** -0.5)
    cf_b_pw2 = nrm((N_B_LAYERS, D_MODEL), 0.01)
    peer_w_q = nrm((DEPTH, D_MODEL, N_RHEADS * D_KEY), D_MODEL ** -0.5)
    peer_sub_keys = nrm((DEPTH, N_RHEADS, 2, N_KEYS, D_HALF), D_HALF ** -0.5)
    peer_u = nrm((DEPTH, N_EXPERTS, D_MODEL), D_MODEL ** -0.5)
    peer_v = nrm((DEPTH, N_EXPERTS, D_MODEL), N_RHEADS ** -0.5)
    return {
        'x_prompt': x_prompt, 'x_sample': x_sample,
        'state_rglru_h': state_rglru_h, 'state_rglru_conv': state_rglru_conv,
        'state_conformer_conv': state_conformer_conv,
        'norm_mix': norm_mix, 'norm_ffn': norm_ffn, 'norm_final': norm_final,
        'rg_w_in': rg_w_in, 'rg_conv_w': rg_conv_w, 'rg_conv_b': rg_conv_b,
        'rg_w_a': rg_w_a, 'rg_b_a': rg_b_a, 'rg_w_i': rg_w_i, 'rg_b_i': rg_b_i,
        'rg_lambda': rg_lambda, 'rg_w_out': rg_w_out,
        'cf_w_pw1': cf_w_pw1, 'cf_b_pw1': cf_b_pw1, 'cf_dw_w': cf_dw_w, 'cf_dw_b': cf_dw_b,
        'cf_ln_g': cf_ln_g, 'cf_ln_b': cf_ln_b, 'cf_w_pw2': cf_w_pw2, 'cf_b_pw2': cf_b_pw2,
        'peer_w_q': peer_w_q, 'peer_sub_keys': peer_sub_keys, 'peer_u': peer_u, 'peer_v': peer_v,
    }

def reference(x_prompt, x_sample, state_rglru_h, state_rglru_conv, state_conformer_conv,
              norm_mix, norm_ffn, norm_final, rg_w_in, rg_conv_w, rg_conv_b, rg_w_a, rg_b_a,
              rg_w_i, rg_b_i, rg_lambda, rg_w_out, cf_w_pw1, cf_b_pw1, cf_dw_w, cf_dw_b,
              cf_ln_g, cf_ln_b, cf_w_pw2, cf_b_pw2, peer_w_q, peer_sub_keys, peer_u, peer_v):
    params = dict(norm_mix=norm_mix, norm_ffn=norm_ffn, norm_final=norm_final,
                  rg_w_in=rg_w_in, rg_conv_w=rg_conv_w, rg_conv_b=rg_conv_b,
                  rg_w_a=rg_w_a, rg_b_a=rg_b_a, rg_w_i=rg_w_i, rg_b_i=rg_b_i,
                  rg_lambda=rg_lambda, rg_w_out=rg_w_out,
                  cf_w_pw1=cf_w_pw1, cf_b_pw1=cf_b_pw1, cf_dw_w=cf_dw_w, cf_dw_b=cf_dw_b,
                  cf_ln_g=cf_ln_g, cf_ln_b=cf_ln_b, cf_w_pw2=cf_w_pw2, cf_b_pw2=cf_b_pw2,
                  peer_w_q=peer_w_q, peer_sub_keys=peer_sub_keys, peer_u=peer_u, peer_v=peer_v)
    dt = x_prompt.dtype
    nbp = x_prompt.shape[0]
    h0_p = jnp.zeros((N_A_LAYERS, nbp, D_RNN), dt)
    rgc0_p = jnp.zeros((N_A_LAYERS, nbp, RG_CONV_W - 1, D_RNN), dt)
    cfc0_p = jnp.zeros((N_B_LAYERS, nbp, CONF_CONV_W - 1, D_CONV), dt)
    y_prompt, p_h, p_rgc, p_cfc = trunk(x_prompt, h0_p, rgc0_p, cfc0_p, params)
    y_sample, s_h, s_rgc, s_cfc = trunk(x_sample, state_rglru_h, state_rglru_conv,
                                        state_conformer_conv, params)
    return (y_prompt, y_sample, p_h, p_rgc, p_cfc, s_h, s_rgc, s_cfc)


_drawn_inputs = setup_inputs


def setup_inputs(seed=0):
    import zlib

    import numpy as np

    out = dict(_drawn_inputs(seed))
    spreads = {}
    factors = {'norm_final': 8.122,
     'rg_b_a': 20.179,
     'rg_b_i': 13.184,
     'cf_b_pw1': 4.516,
     'cf_dw_b': 2.719,
     'cf_ln_g': 2.678,
     'cf_ln_b': 13.548,
     'cf_b_pw2': 10.014}
    for name, (base, spread) in spreads.items():
        noise = np.random.default_rng([zlib.crc32(name.encode()), seed]).standard_normal(out[name].shape)
        drawn = base * np.exp(spread * noise) if base else spread * noise
        out[name] = __import__('jax').numpy.asarray(drawn.astype(out[name].dtype))
    for name, factor in factors.items():
        out[name] = (out[name] * factor).astype(out[name].dtype)
    return out
```

```python
from contextlib import ExitStack

import concourse.bass as bass
from concourse import mybir

ALU = mybir.AluOpType
ACT = mybir.ActivationFunctionType
AX_X = mybir.AxisListType.X
F32 = mybir.dt.float32
F32R = mybir.dt.float32r
BF16 = mybir.dt.bfloat16
U32 = mybir.dt.uint32

P = 128
D = 1024
CH = D // P
TP = 256
NSEQ, SL = 8, 4
TS = NSEQ * SL
T = TP + TS
RG_W, CF_W = 4, 31
HEADS, KEYS, TOPK = 8, 128, 16
GROUPS = 2 * HEADS
PICKS = HEADS * TOPK
TT, NT = 96, 3
EPS = 1e-6
RG_C = 8.0
LOWEST = -3.0e38

SLOTS = 4
LEAD = 3
HT = 64
IN0, IN_N = 0, 16
OUT0, OUT_N = 16, 8
Q0, Q_N = 24, 16
UA0, UA_N = 40, HT
VA0, VA_N = 104, HT // 2
MIX0, MIX_N = 136, 96
VC0, VC_N = 232, HT // 2
VD0, VD_N = 264, HT // 2
SLABS = 296
DEPTH = 2
TOTAL = DEPTH * SLABS
USE_IN, USE_Q, USE_UA, USE_MIX, USES = 0, 8, 16, 48, 80
X_MIX, X_VA, X_VB, X_VC, X_VD = 8, 12, 16, 20, 24

SUM_MIX, SUM_FFN, SUM_MEAN, SUM_VAR, SUM_FINAL = (0, 2), (1, 5), 3, 4, 6
SQ_MIX, SQ_FFN, SQ_VAR, SQ_FINAL = (1, 3), (2, 5), 4, 6
SRC_MIX, SRC_LRU, SRC_FFN = (0, 3 * CH), CH, (2 * CH, 4 * CH + 3)
SRC_CONV, SRC_CENTRED, SRC_SCALED, SRC_FINAL = 4 * CH + 1, 4 * CH + 2, 4 * CH + 3, 5 * CH + 3
PUB_MIX, PUB_OUT, PUB_FFN = (0, 3), (1, 4), (2, 5)
ROUTE_STEPS = 16
CF_STORES = 1 + CH

GTOK = 8
GCH = T // GTOK

COLS, _n = {}, 0
for _name, _w in (("norm_mix", 16), ("norm_ffn", 16), ("norm_final", 8), ("rg_conv_w", 32),
                  ("rg_conv_b", 8), ("rg_b_a", 8), ("rg_b_i", 8), ("rg_lambda", 8),
                  ("cf_b_pw1", 16), ("cf_dw_w", CF_W * 8), ("cf_dw_b", 8), ("cf_ln_g", 8),
                  ("cf_ln_b", 8), ("cf_b_pw2", 8), ("state_h", 64), ("state_conv", 192)):
    COLS[_name] = _n
    _n += _w
NCOL = _n

EXT = TP + RG_W - 1 + NSEQ * (SL + RG_W - 1)
EXT_S = TP + RG_W - 1
ZEXT = TP + CF_W - 1 + NSEQ * (SL + CF_W - 1)
ZEXT_S = TP + CF_W - 1
ZROW = SL + CF_W - 1


def build(nc, x0, stream, cols_d, keys_d, blocks_d, cstate_d, y_d, h_d, rgc_d, cfp_d, cfs_d):
    with ExitStack() as ctx:
        def sb(name, shape, dt=F32):
            return ctx.enter_context(nc.sbuf_tensor(name, shape, dt))

        def sem(name):
            return ctx.enter_context(nc.semaphore(name))

        x = sb("x", [P, CH, T])
        act_hi = sb("act_hi", [P, CH, T], F32R)
        act_lo = sb("act_lo", [P, CH, T], F32R)
        land = sb("land", [P, SLOTS, D])
        w_hi = sb("w_hi", [P, SLOTS, D], F32R)
        w_lo = sb("w_lo", [P, SLOTS, D], F32R)
        hidden = sb("hidden", [P, HT, T])
        g_hi = sb("g_hi", [P, 4, T], F32R)
        g_lo = sb("g_lo", [P, 4, T], F32R)
        work = sb("work", [P, 8448])
        cols = sb("cols", [P, NCOL])
        decay = sb("decay", [P, 2, CH])
        iota = sb("iota", [P, KEYS])
        ident = sb("ident", [P, P])
        ones = sb("ones", [P, P])
        zeros = sb("zeros", [P, T], BF16)
        rstd = sb("rstd", [P, T])
        picks_tok = sb("picks_tok", [P, 3, NT, PICKS])
        picks = sb("picks", [P, 3, T])
        pick_cols = sb("pick_cols", [P, 2, 3, GTOK])
        head_sum = sb("head_sum", [P, NT * HEADS])
        held = sb("held", [P, 8 + ROUTE_STEPS + 1])
        h_last = sb("h_last", [P, CH, 1 + NSEQ])
        rg_last = sb("rg_last", [P, CH, 1 + NSEQ, RG_W - 1])

        flat = hidden[:, :, :].rearrange("p a t -> p (a t)")

        def view(base, lo, *dims):
            n = 1
            for d in dims:
                n *= d
            v = base[:, lo:lo + n]
            names = "abcd"[:len(dims)]
            if len(dims) > 1:
                v = v.rearrange(f"p ({' '.join(names)}) -> p {' '.join(names)}",
                                **dict(zip(names, dims)))
            return v

        def hidden_tile(slot):
            return hidden[:, bass.ds(slot, 1), :].rearrange("p o t -> p (o t)")

        CT = CH * T
        gate = view(flat, 0, CH, T)
        xc = view(flat, CT, CH, T)
        r_h = view(flat, 2 * CT, CH, T)
        i_g = view(flat, 3 * CT, CH, T)
        a_g = view(flat, 4 * CT, CH, T)
        u_g = view(flat, 5 * CT, CH, T)
        ext = view(flat, 6 * CT, CH, EXT)
        z_ext = view(flat, 0, CH, ZEXT)
        cv = view(flat, CH * ZEXT, CH, T)
        sq_cf = view(flat, CH * ZEXT + CT, CH, T)
        glu_gate = view(flat, CH * ZEXT + 2 * CT, 2, T)
        mean = view(flat, CH * ZEXT + 2 * CT + 2 * T, T)
        q_t = view(flat, 0, GROUPS, T)
        SCORES = HT * T - NT * GROUPS * KEYS
        scores = view(flat, SCORES, NT, GROUPS * KEYS)
        U_CLEAR = SCORES // T // SLOTS
        A, B, C, E = 0, 2304, 4352, 6400
        work_f = work[:, :]
        sq = view(work_f, A, CH, T)
        keys = view(work_f, B, GROUPS, KEYS)
        blocks = view(work_f, C, 2, CH, P)
        cstate = view(work_f, C, CH, NSEQ, CF_W - 1)
        conv_prod = view(work_f, E, NSEQ, SL, CF_W)
        s_tile = view(work_f, A, GROUPS, KEYS)
        s_rest = view(work_f, C, GROUPS, KEYS)
        top_v = view(work_f, B, GROUPS, TOPK)
        top_i = view(work_f, B + 256, GROUPS, TOPK).bitcast(U32)
        top_f = view(work_f, B + 512, GROUPS, TOPK)
        best = view(work_f, B + 768, HEADS, TOPK)
        pos = view(work_f, B + 896, HEADS, TOPK).bitcast(U32)
        pos_ab = view(work_f, B + 1024, 2, PICKS).bitcast(U32)
        pos_f = view(work_f, B + 1280, 2, PICKS)
        cand = view(work_f, E, HEADS, TOPK * TOPK)
        cand_rest = view(work_f, A, HEADS, TOPK * TOPK)
        hot = [view(work_f, off, HEADS, TOPK, TOPK) for off in (E, C)]
        onehot_j = view(work_f, A, 2, GTOK, KEYS)
        onehot_i = view(work_f, E, 2, GTOK, HT)

        def hold(engine, k=0):
            if engine.engine == nc.scalar.engine:
                nc.scalar.copy(held[0:1, k:k + 1], ones[0:1, 0:1])
            else:
                nc.vector.tensor_copy(held[0:1, 8 + k:9 + k], ones[0:1, 0:1])

        ps = ctx.enter_context(nc.psum_tensor("ps", [P, 8, 512], F32))
        LIN, NORM, ACC = 0, 2, 4

        landed = [sem(f"landed_{k}") for k in range(SLOTS)]
        w_hi_ready = sem("w_hi_ready")
        w_lo_ready = sem("w_lo_ready")
        slab_used = sem("slab_used")
        evacuated = [sem("evacuated_0"), sem("evacuated_1")]
        loaded = sem("loaded")
        loaded_l = sem("loaded_l")
        consts_ready = sem("consts_ready")
        x_updated = sem("x_updated")
        sq_act = sem("sq_act")
        sq_dve = sem("sq_dve")
        summed = sem("summed")
        std_ready = sem("std_ready")
        src_ready = sem("src_ready")
        silu_ready = sem("silu_ready")
        act_hi_ready = sem("act_hi_ready")
        act_lo_ready = sem("act_lo_ready")
        conv_done = sem("conv_done")
        block_done = sem("block_done")
        block_read = sem("block_read")
        decay_exp = sem("decay_exp")
        decay_ready = sem("decay_ready")
        lru_act = sem("lru_act")
        lru_dve = sem("lru_dve")
        scored = sem("scored")
        scores_copied = sem("scores_copied")
        tile_staged = sem("tile_staged")
        exp_ready = sem("exp_ready")
        picks_ready = sem("picks_ready")
        picks_turned = sem("picks_turned")
        picks_copied = sem("picks_copied")
        onehots_ready = sem("onehots_ready")
        expanded = sem("expanded")
        gated = sem("gated")
        g_hi_ready = sem("g_hi_ready")
        g_lo_ready = sem("g_lo_ready")
        step = sem("step")
        route_step = sem("route_step")
        stored = sem("stored")
        states_ready = sem("states_ready")
        states_out = sem("states_out")

        block = ctx.enter_context(nc.Block())

        def col(name, c, n=1):
            return cols[:, COLS[name] + c:COLS[name] + c + n]

        @block.sync
        def _(sp):
            sp.dma_start(x[:, :, :], x0).then_inc(loaded, 16)
            sp.dma_start(cols[:, :], cols_d).then_inc(loaded, 16)
            for k in range(SLOTS):
                sp.dma_start(land[:, k, :], stream[k]).then_inc(landed[k], 16)
            with sp.Fori(1, TOTAL // SLOTS) as q:
                for k in range(SLOTS):
                    sp.wait_ge(w_lo_ready, 4 * q + (k - 3))
                    sp.dma_start(land[:, k, :], stream[4 * q + k]).then_inc(landed[k], 16)
            for c in range(CH):
                sp.wait_ge(src_ready, SRC_FINAL + c + 1)
                sp.dma_start(y_d[:, c, :], sq[:, c, :]).then_inc(stored, 16)
            sp.wait_ge(stored, 16 * (CH + CF_STORES))
            sp.wait_ge(states_out, 32)

        @block.gpsimd
        def _(pool):
            nc.gpsimd.memset(ones[:, :], 1.0).then_inc(consts_ready, 1)
            nc.gpsimd.memset(zeros[:, :], 0.0).then_inc(consts_ready, 1)
            nc.gpsimd.memset(ident[:, :], 0.0).then_inc(consts_ready, 1)
            nc.gpsimd.memset(blocks, 0.0).then_inc(consts_ready, 1)
            nc.gpsimd.iota(iota[:, :], pattern=[[1, KEYS]], base=0, channel_multiplier=0,
                           allow_small_or_imprecise_dtypes=True).then_inc(consts_ready, 1)
            pool.wait_ge(consts_ready, 5)
            nc.gpsimd.affine_select(out=ident[:, :], in_=ident[:, :], compare_op=ALU.not_equal,
                                    fill=1.0, base=0, pattern=[[-1, P]],
                                    channel_multiplier=1).then_inc(consts_ready, 1)
            with pool.Fori(0, TOTAL // SLOTS) as q:
                for k in range(SLOTS):
                    pool.wait_ge(w_hi_ready, 4 * q + (k + 1))
                    nc.gpsimd.tensor_tensor(w_lo[:, k, :], land[:, k, :], w_hi[:, k, :].bitcast(F32),
                                            ALU.subtract).then_inc(w_lo_ready, 1)

        @block.scalar
        def _(act):
            def split(q, m):
                q, m = q + m // SLOTS, m % SLOTS
                first = isinstance(q, int) and q == 0
                act.wait_ge(landed[m], 16 * q + 16)
                if not first:
                    act.wait_ge(slab_used, 4 * q + (m - 3))
                nc.scalar.copy(w_hi[:, m, :], land[:, m, :]).then_inc(w_hi_ready, 1)

            def split_ahead(q, m):
                if isinstance(q, int) and 4 * q + m + LEAD >= TOTAL:
                    return
                split(q, m + LEAD)

            def squares(x_count):
                if x_count:
                    act.wait_ge(x_updated, x_count)
                else:
                    act.wait_ge(loaded, 32)
                nc.scalar.activation(sq[:, 0:4, :], x[:, 0:4, :], ACT.Square).then_inc(sq_act, 1)

            def root(n):
                act.wait_ge(summed, n + 1)
                nc.scalar.activation(rstd[:, :], ps[:, NORM, 0:T], ACT.Sqrt, bias=EPS,
                                     scale=1.0 / D).then_inc(std_ready, 1)

            def publish(ready, base):
                for c in range(CH):
                    act.wait_ge(ready, base + c + 1)
                    nc.scalar.copy(act_hi[:, c, :], sq[:, c, :]).then_inc(act_hi_ready, 1)

            def gated_hi(slot, ring):
                nc.scalar.copy(g_hi[:, ring, :], hidden_tile(slot)).then_inc(g_hi_ready, 1)

            def layer(L):
                base = L * SLABS
                use = L * USES

                def lin_done(n):
                    act.wait_ge(slab_used, base + n + 1)

                squares(L * X_VD)
                root(SUM_MIX[L])
                publish(src_ready, SRC_MIX[L])
                if L == 0:
                    for n in range(IN_N):
                        split_ahead(base // 4, IN0 + n)
                        lin_done(IN0 + n)
                        c = n % CH
                        if n < CH:
                            nc.scalar.copy(ext[:, c, RG_W - 1:EXT_S], ps[:, LIN + n % 2, 0:TP])
                            nc.scalar.copy(
                                ext[:, c, EXT_S:EXT].rearrange("p (s w) -> p s w", s=NSEQ)[:, :, RG_W - 1:],
                                ps[:, LIN + n % 2, TP:T].rearrange("p (s w) -> p s w", s=NSEQ),
                            ).then_inc(evacuated[n % 2], 1)
                        else:
                            nc.scalar.activation(gate[:, c, :], ps[:, LIN + n % 2, 0:T],
                                                 ACT.Gelu_apprx_tanh).then_inc(evacuated[n % 2], 1)
                    for c in range(CH):
                        for m, (dst, bias) in enumerate(((r_h, "rg_b_a"), (i_g, "rg_b_i"))):
                            act.wait_ge(block_done, 2 * c + m + 1)
                            nc.scalar.activation(dst[:, c, :], ps[:, NORM + m, 0:T], ACT.Sigmoid,
                                                 bias=col(bias, c)).then_inc(block_read, 1)
                    act.wait_ge(decay_ready, 1)
                    act.wait_ge(block_read, 2 * CH)
                    for c in range(CH):
                        nc.scalar.activation(a_g[:, c, :], r_h[:, c, :], ACT.Exp,
                                             scale=decay[:, 0, c:c + 1]).then_inc(lru_act, 1)
                        nc.scalar.activation(u_g[:, c, :], r_h[:, c, :], ACT.Tanh,
                                             scale=decay[:, 1, c:c + 1]).then_inc(lru_act, 1)
                    for half in range(2):
                        act.wait_ge(lru_dve, half + 1)
                        part = u_g[:, 4 * half:4 * half + 4, :]
                        nc.scalar.activation(part, part, ACT.Sqrt).then_inc(lru_act, 1)
                    publish(src_ready, SRC_LRU)
                else:
                    for n in range(IN_N):
                        split_ahead(base // 4, IN0 + n)
                        if n % 2:
                            continue
                        lin_done(IN0 + n)
                        c = n // 2
                        if c >= 2:
                            act.wait_ge(evacuated[1], use + USE_IN + c - 1)
                        nc.scalar.activation(glu_gate[:, c % 2, :], ps[:, LIN, 0:T], ACT.Sigmoid,
                                             bias=col("cf_b_pw1", CH + c)).then_inc(evacuated[0], 1)
                    act.wait_ge(evacuated[1], use + USE_Q)
                    act.dma_start(cfp_d, z_ext[:, :, ZEXT_S - (CF_W - 1):ZEXT_S]).then_inc(stored, 16)
                    for c in range(CH):
                        act.dma_start(cfs_d[:, c], z_ext[:, c, ZEXT_S:ZEXT].rearrange(
                            "p (s w) -> p s w", s=NSEQ)[:, :, SL:]).then_inc(stored, 16)
                    act.wait_ge(summed, SUM_MEAN + 1)
                    nc.scalar.activation(mean, ps[:, NORM, 0:T], ACT.Copy,
                                         scale=1.0 / D).then_inc(std_ready, 1)
                    act.wait_ge(src_ready, SRC_CENTRED)
                    nc.scalar.activation(sq_cf[:, 0:4, :], cv[:, 0:4, :], ACT.Square).then_inc(sq_act, 1)
                    root(SUM_VAR)
                    act.wait_ge(src_ready, SRC_SCALED)
                    for c in range(CH):
                        nc.scalar.activation(sq[:, c, :], cv[:, c, :], ACT.Silu,
                                             bias=col("cf_ln_b", c),
                                             scale=col("cf_ln_g", c)).then_inc(silu_ready, 1)
                    publish(silu_ready, 0)
                for n in range(OUT_N):
                    split_ahead(base // 4, OUT0 + n)
                if L == 0:
                    act.wait_ge(states_ready, 3 + CH)
                    act.dma_start(h_d, h_last[:, :, :]).then_inc(states_out, 16)
                    act.dma_start(rgc_d, rg_last[:, :, :, :]).then_inc(states_out, 16)
                squares(L * X_VD + X_MIX)
                root(SUM_FFN[L])
                publish(src_ready, SRC_FFN[L])
                if L == 1:
                    act.wait_ge(stored, 16 * CF_STORES)
                for n in range(Q_N):
                    split_ahead(base // 4, Q0 + n)
                    lin_done(Q0 + n)
                    nc.scalar.copy(q_t[:, n, :], ps[:, LIN + n % 2, 0:T]).then_inc(evacuated[n % 2], 1)

                def u_tile(slot, bank):
                    nc.scalar.activation(hidden_tile(slot), ps[:, bank, 0:T],
                                         ACT.Gelu_apprx_tanh).then_inc(evacuated[bank], 1)

                def u_steps(q):
                    for k in range(4):
                        split_ahead(base // 4 + UA0 // 4 + q, k)
                        act.wait_ge(slab_used, 4 * q + (base + UA0 + k + 1))
                        hold(act, k)
                        u_tile(4 * q + k, k % 2)

                with act.Fori(0, U_CLEAR) as q:
                    u_steps(q)
                act.wait_ge(tile_staged, NT * (L + 1))
                with act.Fori(U_CLEAR, HT // 4) as q:
                    u_steps(q)

                act.wait_ge(route_step, ROUTE_STEPS * NT * (L + 1))
                nc.scalar.activation(picks_tok[0:TT, 2, :, :], picks_tok[0:TT, 2, :, :],
                                     ACT.Exp).then_inc(exp_ready, 1)
                for kind in range(3):
                    act.wait_ge(picks_turned, 3 * L + kind + 1)
                    nc.scalar.copy(picks[:, kind, :], ps[:, ACC + kind, 0:T]).then_inc(picks_copied, 1)

                def v_steps(start, q):
                    for k in range(4):
                        act.wait_ge(slab_used, 4 * q + (base + start + k - 1))
                        for ii in range(2):
                            gated_hi(8 * q + (2 * k + ii), (2 * k + ii) % 4)
                        split_ahead(base // 4 + start // 4 + q, k)

                act.wait_ge(gated, GCH * (2 * L + 1))
                with act.Fori(0, VA_N // 4) as q:
                    v_steps(VA0, q)

                def mix_steps(q, last):
                    for k in range(4):
                        m = 3 * k
                        Q = base // 4 + MIX0 // 4 + 3 * q
                        split_ahead(Q, m)
                        split_ahead(Q, m + 1)
                        if not (last and k == 3):
                            for ii in range(2):
                                gated_hi(8 * q + (2 * k + 2 + ii), (2 * k + 2 + ii) % 4)
                        for r in range(2):
                            if r:
                                split_ahead(Q, m + 2)
                            act.wait_ge(slab_used, 12 * q + (base + MIX0 + m + r + 2))
                            hold(act, 2 * k + r)
                            u_tile(8 * q + (2 * k + r), r)

                act.wait_ge(slab_used, base + MIX0 - 1)
                for ii in range(2):
                    gated_hi(ii, ii)
                with act.Fori(0, MIX_N // 12 - 1) as q:
                    mix_steps(q, False)
                mix_steps(MIX_N // 12 - 1, True)

                act.wait_ge(gated, GCH * (2 * L + 2))
                for start in (VC0, VD0):
                    if L == DEPTH - 1 and start == VD0:
                        with act.Fori(0, VD_N // 4 - 1) as q:
                            v_steps(start, q)
                        v_steps(start, VD_N // 4 - 1)
                    else:
                        with act.Fori(0, VD_N // 4) as q:
                            v_steps(start, q)

            act.wait_ge(consts_ready, 4)
            act.dma_start(keys, keys_d[0]).then_inc(loaded_l, 16)
            for m in range(2):
                for b in range(2):
                    act.dma_start(blocks[64 * b:64 * b + 64, m, :, 64 * b:64 * b + 64],
                                  blocks_d[m, b]).then_inc(loaded_l, 16)
            for m in range(LEAD):
                split(0, m)
            act.wait_ge(decay_exp, 1)
            nc.scalar.activation(decay[:, 1, :], decay[:, 0, :], ACT.Exp).then_inc(decay_exp, 1)
            layer(0)
            act.dma_start(keys, keys_d[1]).then_inc(loaded_l, 16)
            act.dma_start(cstate, cstate_d).then_inc(loaded_l, 16)
            layer(1)
            squares(DEPTH * X_VD)
            root(SUM_FINAL)

        @block.tensor
        def _(pe):
            def column_sum(n, src, waits):
                for s, v in waits:
                    pe.wait_ge(s, v)
                for c in range(CH):
                    mm = nc.tensor.matmul(ps[:, NORM, 0:T], ones[:, :], src[:, c, :],
                                          start=(c == 0), stop=(c == CH - 1))
                mm.then_inc(summed, 1)

            def three_terms(out, wsl, slot, hi, lo, start, stop, **kw):
                nc.tensor.matmul(out, w_hi[:, slot, wsl], hi, start=start, stop=False, **kw)
                nc.tensor.matmul(out, w_lo[:, slot, wsl], hi, start=False, stop=False, **kw)
                return nc.tensor.matmul(out, w_hi[:, slot, wsl], lo, start=False, stop=stop, **kw)

            def linear(q, m, bank, read, count, published=None):
                q, m = q + m // SLOTS, m % SLOTS
                pe.wait_ge(w_lo_ready, 4 * q + (m + 1))
                if not (isinstance(count, int) and count == 0):
                    pe.wait_ge(read, count)
                for c in range(CH):
                    if published is not None:
                        pe.wait_ge(act_lo_ready, published * CH + c + 1)
                    mm = three_terms(ps[:, LIN + bank, 0:T], slice(c * P, c * P + P), m,
                                     act_hi[:, c, :], act_lo[:, c, :], c == 0, c == CH - 1)
                mm.then_inc(slab_used, 1)

            def v_slab(q, m, ring, tiles):
                q, m = q + m // SLOTS, m % SLOTS
                pe.wait_ge(w_lo_ready, 4 * q + (m + 1))
                for ii in range(2):
                    pe.wait_ge(g_lo_ready, tiles + (ii + 1))
                    for c in range(4):
                        mm = three_terms(ps[:, ACC + c, 0:T], slice(ii * 512 + c * P, ii * 512 + c * P + P), m,
                                         g_hi[:, ring + ii, :], g_lo[:, ring + ii, :], False, False,
                                         skip_group_check=True)
                mm.then_inc(slab_used, 1)

            def clear_acc(x_count):
                for c in range(4):
                    pe.wait_ge(x_updated, x_count + (c - 3))
                    nc.tensor.matmul(ps[:, ACC + c, 0:T], zeros[:, 0:P], zeros[:, :], start=True,
                                     stop=False, skip_group_check=True)

            def expand_gates(half_index):
                first = GCH * half_index

                def chunk(g, buf, head):
                    pe.wait_ge(onehots_ready, g + (first + 1))
                    if not head:
                        pe.wait_ge(gated, g + (first - 1))
                    for t in range(GTOK):
                        mm = nc.tensor.matmul(ps[:, NORM + buf, t * HT:(t + 1) * HT],
                                              onehot_j[:, buf, t, :], onehot_i[:, buf, t, :],
                                              start=True, stop=True)
                    mm.then_inc(expanded, 1)

                chunk(0, 0, True)
                chunk(1, 1, True)
                with pe.Fori(1, GCH // 2) as q:
                    chunk(2 * q, 0, False)
                    chunk(2 * q + 1, 1, False)

            def layer(L):
                base = L * SLABS
                use = L * USES
                q0 = base // 4
                column_sum(SUM_MIX[L], sq, ((sq_act, SQ_MIX[L]), (sq_dve, SQ_MIX[L])))
                for n in range(IN_N):
                    linear(q0, IN0 + n, n % 2, evacuated[n % 2], use + USE_IN + n // 2,
                           PUB_MIX[L] if n == 0 else None)
                if L == 0:
                    pe.wait_ge(loaded_l, 16 * 5)
                    for c in range(CH):
                        pe.wait_ge(conv_done, c + 1)
                        for m in range(2):
                            if c:
                                pe.wait_ge(block_read, 2 * c + m - 1)
                            nc.tensor.matmul(ps[:, NORM + m, 0:T], blocks[:, m, c, :], xc[:, c, :],
                                             start=True, stop=True).then_inc(block_done, 1)
                else:
                    column_sum(SUM_MEAN, cv, ((src_ready, SRC_CONV),))
                    column_sum(SUM_VAR, sq_cf, ((sq_act, SQ_VAR), (sq_dve, SQ_VAR)))
                for n in range(OUT_N):
                    if n < 2:
                        linear(q0, OUT0 + n, n, evacuated[n], use + USE_Q, PUB_OUT[L] if n == 0 else None)
                    else:
                        linear(q0, OUT0 + n, n % 2, x_updated, L * X_VD + n - 1)
                column_sum(SUM_FFN[L], sq, ((sq_act, SQ_FFN[L]), (sq_dve, SQ_FFN[L])))
                pe.wait_ge(x_updated, L * X_VD + X_MIX)
                for n in range(Q_N):
                    linear(q0, Q0 + n, n % 2, evacuated[n % 2], use + USE_Q + n // 2,
                           PUB_FFN[L] if n == 0 else None)
                pe.wait_ge(evacuated[0], use + USE_UA)
                pe.wait_ge(evacuated[1], use + USE_UA)
                pe.wait_ge(loaded_l, 16 * (5, 7)[L])
                for u in range(4 * NT):
                    tile, b = u // 4, u % 4
                    if u >= 6:
                        pe.wait_ge(scores_copied, 4 * NT * L + u - 5)
                    for g in range(4):
                        mm = nc.tensor.matmul(ps[0:TT, 2 + u % 6, g * KEYS:(g + 1) * KEYS],
                                              q_t[:, 4 * b + g, tile * TT:(tile + 1) * TT],
                                              keys[:, 4 * b + g, :], start=True, stop=True)
                    mm.then_inc(scored, 1)
                with pe.Fori(0, UA_N // 4) as q:
                    for k in range(4):
                        linear(q0 + UA0 // 4 + q, k, k % 2, evacuated[k % 2], 2 * q + (use + USE_UA + k // 2))
                pe.wait_ge(scores_copied, 4 * NT * (L + 1))
                for kind in range(3):
                    pe.wait_ge(picks_ready, L + 1)
                    for tile in range(NT):
                        mm = nc.tensor.transpose(ps[:, ACC + kind, tile * TT:(tile + 1) * TT],
                                                 picks_tok[0:TT, kind, tile, :], ident[0:TT, 0:TT])
                    mm.then_inc(picks_turned, 1)
                expand_gates(2 * L)
                pe.wait_ge(picks_copied, 3 * L + 3)
                clear_acc(L * X_VD + X_MIX)
                with pe.Fori(0, VA_N // 4) as q:
                    for k in range(4):
                        v_slab(q0 + VA0 // 4 + q, k, 2 * (k % 2), 8 * q + (256 * L + 2 * k))
                clear_acc(L * X_VD + X_VA)
                with pe.Fori(0, MIX_N // 12) as q:
                    for k in range(4):
                        Q = q0 + MIX0 // 4 + 3 * q
                        v_slab(Q, 3 * k, 2 * (k % 2), 8 * q + (256 * L + 64 + 2 * k))
                        for r in range(2):
                            linear(Q, 3 * k + 1 + r, r, evacuated[r], 4 * q + (use + USE_MIX + k))
                expand_gates(2 * L + 1)
                for n, start in enumerate((VC0, VD0)):
                    clear_acc(L * X_VD + (X_VB, X_VC)[n])
                    with pe.Fori(0, VC_N // 4) as q:
                        for k in range(4):
                            v_slab(q0 + start // 4 + q, k, 2 * (k % 2),
                                   8 * q + (256 * L + 128 + 64 * n + 2 * k))

            pe.wait_ge(consts_ready, 6)
            layer(0)
            layer(1)
            column_sum(SUM_FINAL, sq, ((sq_act, SQ_FINAL), (sq_dve, SQ_FINAL)))

        @block.vector
        def _(dve):
            steps = [0]
            V = nc.vector

            def did(ins):
                steps[0] += 1
                ins.then_inc(step, 1)

            def settle():
                dve.wait_ge(step, steps[0])

            def squares(x_count):
                if x_count:
                    dve.wait_ge(x_updated, x_count)
                else:
                    dve.wait_ge(loaded, 32)
                V.tensor_tensor(sq[:, 4:8, :], x[:, 4:8, :], x[:, 4:8, :], ALU.mult).then_inc(sq_dve, 1)

            def invert(n):
                dve.wait_ge(std_ready, n + 1)
                did(V.reciprocal(rstd[:, :], rstd[:, :]))
                settle()

            def normed(n, name, c0):
                invert(n)
                for c in range(CH):
                    V.scalar_tensor_tensor(out=sq[:, c, :], in0=x[:, c, :], scalar=col(name, c0 + c),
                                           in1=rstd[:, :], op0=ALU.mult,
                                           op1=ALU.mult).then_inc(src_ready, 1)

            def publish(n):
                for c in range(CH):
                    dve.wait_ge(act_hi_ready, n * CH + c + 1)
                    V.tensor_tensor(act_lo[:, c, :], sq[:, c, :], act_hi[:, c, :].bitcast(F32),
                                    ALU.subtract).then_inc(act_lo_ready, 1)

            def decay_columns():
                lam, s, e = col("rg_lambda", 0, CH), decay[:, 0, :], decay[:, 1, :]
                t = [view(work_f, E + CH * k, CH) for k in range(5)]
                did(V.tensor_scalar(t[0], lam, -1.0, None, ALU.mult))
                settle()
                did(V.tensor_tensor(t[1], lam, t[0], ALU.max))
                settle()
                V.tensor_scalar(s, t[1], -1.0, None, ALU.mult).then_inc(decay_exp, 1)
                dve.wait_ge(decay_exp, 2)
                did(V.tensor_scalar(t[1], e, 2.0, None, ALU.add))
                settle()
                did(V.reciprocal(t[2], t[1]))
                settle()
                did(V.tensor_tensor(t[1], e, t[2], ALU.mult))
                settle()
                did(V.tensor_tensor(t[2], t[1], t[1], ALU.mult))
                did(V.memset(t[3], 1.0 / 19))
                settle()
                for odd in range(17, 0, -2):
                    did(V.tensor_tensor(t[4], t[3], t[2], ALU.mult))
                    settle()
                    did(V.tensor_scalar(t[3], t[4], 1.0 / odd, None, ALU.add))
                    settle()
                did(V.tensor_tensor(t[4], t[3], t[1], ALU.mult))
                did(V.tensor_scalar(t[2], t[0], 0.0, None, ALU.max))
                settle()
                did(V.scalar_tensor_tensor(out=t[3], in0=t[4], scalar=2.0, in1=t[2],
                                           op0=ALU.mult, op1=ALU.add))
                settle()
                did(V.tensor_scalar(decay[:, 0, :], t[3], -RG_C, None, ALU.mult))
                V.tensor_scalar(decay[:, 1, :], t[3], RG_C, None, ALU.mult).then_inc(decay_ready, 1)

            def seqs(v):
                return v.rearrange("p (s w) -> p s w", s=NSEQ)

            def rg_mixer():
                for c in range(CH):
                    dve.wait_ge(evacuated[c % 2], USE_IN + c // 2 + 1)
                    for k in range(RG_W):
                        w = col("rg_conv_w", k * CH + c)
                        pairs = ((xc[:, c, 0:TP], ext[:, c, k:k + TP]),
                                 (seqs(xc[:, c, TP:T]), seqs(ext[:, c, EXT_S:EXT])[:, :, k:k + SL]))
                        for n, (dst, src) in enumerate(pairs):
                            if k == 0:
                                ins = V.tensor_scalar(dst, src, w, col("rg_conv_b", c), ALU.mult, ALU.add)
                            else:
                                ins = V.scalar_tensor_tensor(out=dst, in0=src, scalar=w, in1=dst,
                                                             op0=ALU.mult, op1=ALU.add)
                            if k == RG_W - 1 and n == 1:
                                ins.then_inc(conv_done, 1)
                            else:
                                did(ins)
                        if k < RG_W - 1:
                            settle()
                V.tensor_copy(rg_last[:, :, 0, :], ext[:, :, TP:EXT_S]).then_inc(states_ready, 1)
                for c in range(CH):
                    V.tensor_copy(rg_last[:, c, 1:, :],
                                  seqs(ext[:, c, EXT_S:EXT])[:, :, SL:]).then_inc(states_ready, 1)
                dve.wait_ge(conv_done, CH)
                for c in range(CH):
                    dve.wait_ge(block_read, 2 * c + 2)
                    did(V.tensor_tensor(i_g[:, c, :], i_g[:, c, :], xc[:, c, :], ALU.mult))
                tmp = r_h
                for half in range(2):
                    h4 = slice(4 * half, 4 * half + 4)
                    dve.wait_ge(lru_act, 2 * CH)
                    did(V.tensor_tensor(tmp[:, h4, :], a_g[:, h4, :], a_g[:, h4, :], ALU.mult))
                    settle()
                    V.scalar_tensor_tensor(out=u_g[:, h4, :], in0=tmp[:, h4, :], scalar=1.0,
                                           in1=u_g[:, h4, :], op0=ALU.add,
                                           op1=ALU.mult).then_inc(lru_dve, 1)
                h0 = col("state_h", 0, 64).rearrange("p (c s) -> p c s", c=CH)
                carry = view(work_f, E, CH, NSEQ)
                a_first = a_g[:, :, TP:T].rearrange("p c (s w) -> p c s w", s=NSEQ)[:, :, :, 0]
                u_first = u_g[:, :, TP:T].rearrange("p c (s w) -> p c s w", s=NSEQ)[:, :, :, 0]
                for half in range(2):
                    h4 = slice(4 * half, 4 * half + 4)
                    did(V.tensor_tensor(carry[:, h4, :], a_first[:, h4, :], h0[:, h4, :], ALU.mult))
                    dve.wait_ge(lru_act, 2 * CH + half + 1)
                    did(V.tensor_tensor(u_g[:, h4, :], u_g[:, h4, :], i_g[:, h4, :], ALU.mult))
                    settle()
                    did(V.tensor_tensor(u_first[:, h4, :], u_first[:, h4, :], carry[:, h4, :], ALU.add))
                    did(V.memset(a_first[:, h4, :], 0.0))
                    did(V.memset(a_g[:, h4, 0:1], 0.0))
                    settle()
                    did(V.tensor_tensor_scan(r_h[:, h4, :].rearrange("p c t -> p (c t)"),
                                             a_g[:, h4, :].rearrange("p c t -> p (c t)"),
                                             u_g[:, h4, :].rearrange("p c t -> p (c t)"),
                                             0.0, ALU.mult, ALU.add))
                    if half == 0:
                        dve.wait_ge(evacuated[0], USE_Q)
                        dve.wait_ge(evacuated[1], USE_Q)
                    settle()
                    for c in range(4 * half, 4 * half + 4):
                        V.tensor_tensor(sq[:, c, :], r_h[:, c, :], gate[:, c, :],
                                        ALU.mult).then_inc(src_ready, 1)
                publish(PUB_OUT[0])
                V.tensor_copy(h_last[:, :, 0:1], r_h[:, :, TP - 1:TP]).then_inc(states_ready, 1)
                V.tensor_copy(h_last[:, :, 1:],
                              r_h[:, :, TP:T].rearrange("p c (s w) -> p c s w", s=NSEQ)[:, :, :, SL - 1]
                              ).then_inc(states_ready, 1)

            def conformer():
                for c in range(CH):
                    dve.wait_ge(slab_used, SLABS + IN0 + 2 * c + 2)
                    dve.wait_ge(evacuated[0], USES + USE_IN + c + 1)
                    b = col("cf_b_pw1", c)
                    did(V.scalar_tensor_tensor(out=z_ext[:, c, CF_W - 1:ZEXT_S], in0=ps[:, LIN + 1, 0:TP],
                                               scalar=b, in1=glu_gate[:, c % 2, 0:TP],
                                               op0=ALU.add, op1=ALU.mult))
                    V.scalar_tensor_tensor(
                        out=seqs(z_ext[:, c, ZEXT_S:ZEXT])[:, :, CF_W - 1:],
                        in0=seqs(ps[:, LIN + 1, TP:T]), scalar=b, in1=seqs(glu_gate[:, c % 2, TP:T]),
                        op0=ALU.add, op1=ALU.mult).then_inc(evacuated[1], 1)
                    settle()
                    dve.wait_ge(evacuated[1], USES + USE_IN + c + 1)
                    wk = cols[:, COLS["cf_dw_w"]:COLS["cf_dw_w"] + CF_W * CH].rearrange(
                        "p (k c) -> p c k", c=CH)[:, c, :]
                    zs = z_ext[:, c, ZEXT_S:ZEXT]
                    for t in range(SL):
                        did(V.tensor_tensor(conv_prod[:, :, t, :], seqs(zs)[:, :, t:t + CF_W],
                                            wk.unsqueeze(1).to_broadcast([P, NSEQ, CF_W]), ALU.mult))
                    dst = cv[:, c, 0:TP]
                    did(V.tensor_scalar(dst, z_ext[:, c, 0:TP], col("cf_dw_w", c), col("cf_dw_b", c),
                                        ALU.mult, ALU.add))
                    settle()
                    did(V.tensor_reduce(seqs(cv[:, c, TP:T]), conv_prod, AX_X, ALU.add))
                    for k in range(1, CF_W):
                        did(V.scalar_tensor_tensor(out=dst, in0=z_ext[:, c, k:k + TP],
                                                   scalar=col("cf_dw_w", k * CH + c), in1=dst,
                                                   op0=ALU.mult, op1=ALU.add))
                        settle()
                    ins = V.tensor_scalar(cv[:, c, TP:T], cv[:, c, TP:T], col("cf_dw_b", c), None, ALU.add)
                    if c < CH - 1:
                        did(ins)
                    else:
                        ins.then_inc(src_ready, 1)
                dve.wait_ge(std_ready, SUM_MEAN + 1)
                dve.wait_ge(src_ready, SRC_CONV)
                V.tensor_tensor(cv, cv, mean.unsqueeze(1).to_broadcast([P, CH, T]),
                                ALU.subtract).then_inc(src_ready, 1)
                dve.wait_ge(src_ready, SRC_CENTRED)
                V.tensor_tensor(sq_cf[:, 4:8, :], cv[:, 4:8, :], cv[:, 4:8, :], ALU.mult).then_inc(sq_dve, 1)
                invert(SUM_VAR)
                V.tensor_tensor(cv, cv, rstd[:, :].unsqueeze(1).to_broadcast([P, CH, T]),
                                ALU.mult).then_inc(src_ready, 1)
                publish(PUB_OUT[1])

            def route(L):
                for u in range(4 * NT):
                    dve.wait_ge(scored, 4 * NT * L + u + 1)
                    tile, b = u // 4, u % 4
                    V.tensor_copy(scores[0:TT, tile, 512 * b:512 * b + 512],
                                  ps[0:TT, 2 + u % 6, :]).then_inc(scores_copied, 1)
                dve.wait_ge(scores_copied, 4 * NT * (L + 1))
                with dve.Fori(0, NT) as tile:
                    n = [0]
                    start = ROUTE_STEPS * (tile + NT * L)

                    def tile_did(ins):
                        n[0] += 1
                        ins.then_inc(route_step, 1)

                    def tile_settle():
                        dve.wait_ge(route_step, start + n[0])
                        hold(dve, n[0])

                    r = slice(0, TT)
                    V.tensor_copy(work[r, A:A + GROUPS * KEYS], scores[r, bass.ds(tile, 1), :].rearrange(
                        "p o k -> p (o k)")).then_inc(tile_staged, 1)
                    dve.wait_ge(tile_staged, tile + (NT * L + 1))
                    hold(dve)
                    for g in range(GROUPS):
                        ins = V.max(top_v[r, g, 0:8], s_tile[r, g, :])
                    tile_did(ins)
                    tile_settle()
                    for g in range(GROUPS):
                        V.match_replace(s_rest[r, g, :], top_v[r, g, 0:8], s_tile[r, g, :], LOWEST)
                        ins = V.max_index(top_i[r, g, 0:8], top_v[r, g, 0:8], s_tile[r, g, :])
                    tile_did(ins)
                    tile_settle()
                    for g in range(GROUPS):
                        ins = V.max(top_v[r, g, 8:16], s_rest[r, g, :])
                    tile_did(ins)
                    tile_settle()
                    for g in range(GROUPS):
                        V.max_index(top_i[r, g, 8:16], top_v[r, g, 8:16], s_rest[r, g, :])
                    tv = top_v[r].rearrange("p (h two) k -> p h two k", two=2)
                    tile_did(V.tensor_tensor(cand[r].rearrange("p h (a b) -> p h a b", a=TOPK),
                                        tv[:, :, 0, :].unsqueeze(3).to_broadcast([TT, HEADS, TOPK, TOPK]),
                                        tv[:, :, 1, :].unsqueeze(2).to_broadcast([TT, HEADS, TOPK, TOPK]),
                                        ALU.add))
                    tile_settle()
                    V.tensor_copy(top_f[r], top_i[r])
                    for h in range(HEADS):
                        ins = V.max(best[r, h, 0:8], cand[r, h, :])
                    tile_did(ins)
                    tile_settle()
                    for h in range(HEADS):
                        V.match_replace(cand_rest[r, h, :], best[r, h, 0:8], cand[r, h, :], LOWEST)
                        ins = V.max_index(pos[r, h, 0:8], best[r, h, 0:8], cand[r, h, :])
                    tile_did(ins)
                    tile_settle()
                    for h in range(HEADS):
                        ins = V.max(best[r, h, 8:16], cand_rest[r, h, :])
                    tile_did(ins)
                    tile_settle()
                    for h in range(HEADS):
                        V.max_index(pos[r, h, 8:16], best[r, h, 8:16], cand_rest[r, h, :])
                    pk = picks_tok[r, 2, bass.ds(tile, 1), :].rearrange("p o (h k) -> p (o h) k", h=HEADS)
                    tile_did(V.tensor_tensor(pk, best[r], best[r, :, 0:1].to_broadcast([TT, HEADS, TOPK]),
                                        ALU.subtract))
                    tile_settle()
                    posf = pos[r].rearrange("p h k -> p (h k)")
                    V.tensor_scalar(pos_ab[r, 0, :], posf, 4, None, ALU.logical_shift_right)
                    tile_did(V.tensor_scalar(pos_ab[r, 1, :], posf, 15, None, ALU.bitwise_and))
                    tile_settle()
                    tile_did(V.tensor_copy(pos_f[r], pos_ab[r]))
                    tile_settle()
                    for s in range(2):
                        pf = pos_f[r, s, :].rearrange("p (h k) -> p h k", h=HEADS)
                        tile_did(V.tensor_tensor(
                            hot[s][r], pf.unsqueeze(3).to_broadcast([TT, HEADS, TOPK, TOPK]),
                            iota[r, 0:TOPK].unsqueeze(1).unsqueeze(1).to_broadcast([TT, HEADS, TOPK, TOPK]),
                            ALU.is_equal))
                    tile_settle()
                    tf = top_f[r].rearrange("p (h two) k -> p h two k", two=2)
                    for s in range(2):
                        tile_did(V.tensor_tensor(
                            hot[s][r], hot[s][r],
                            tf[:, :, s, :].unsqueeze(2).to_broadcast([TT, HEADS, TOPK, TOPK]), ALU.mult))
                    tile_settle()
                    for s in range(2):
                        tile_did(V.tensor_reduce(
                            picks_tok[r, s, bass.ds(tile, 1), :].rearrange("p o k -> p (o k)"),
                            hot[s][r].rearrange("p h k a -> p (h k) a"), AX_X, ALU.add))
                    tile_settle()
                    assert n[0] == ROUTE_STEPS, n[0]
                gates = picks_tok[0:TT, 2, :, :].rearrange("p t (h k) -> p (t h) k", h=HEADS)
                dve.wait_ge(exp_ready, L + 1)
                did(V.tensor_reduce(head_sum[0:TT, :], gates, AX_X, ALU.add))
                settle()
                did(V.reciprocal(head_sum[0:TT, :], head_sum[0:TT, :]))
                settle()
                V.tensor_tensor(gates, gates, head_sum[0:TT, :].unsqueeze(2).to_broadcast(
                    [TT, NT * HEADS, TOPK]), ALU.mult).then_inc(picks_ready, 1)

            def expand_gates(half_index, half):
                first = GCH * half_index
                seen = steps[0]
                steps[0] += GCH

                def onehots(g, buf):
                    if not (isinstance(g, int) and first + g < 2):
                        dve.wait_ge(expanded, g + (first - 1))
                    V.tensor_copy(pick_cols[:, buf, :, :],
                                  picks[:, :, bass.ds(g * GTOK, GTOK)]).then_inc(step, 1)
                    dve.wait_ge(step, g + (seen + 1))
                    for t in range(GTOK):
                        V.tensor_scalar(onehot_j[:, buf, t, :], iota[:, :], pick_cols[:, buf, 1, t:t + 1],
                                        None, ALU.is_equal)
                        ins = V.tensor_scalar(onehot_i[:, buf, t, :], iota[:, half * HT:(half + 1) * HT],
                                              pick_cols[:, buf, 0, t:t + 1],
                                              pick_cols[:, buf, 2, t:t + 1], ALU.is_equal, ALU.mult)
                    ins.then_inc(onehots_ready, 1)

                def apply(g, buf):
                    dve.wait_ge(expanded, g + (first + 1))
                    tok = hidden[:, :, bass.ds(g * GTOK, GTOK)]
                    V.tensor_tensor(tok, ps[:, NORM + buf, :].rearrange("p (t i) -> p i t", t=GTOK), tok,
                                    ALU.mult).then_inc(gated, 1)

                onehots(0, 0)
                onehots(1, 1)
                apply(0, 0)
                with dve.Fori(1, GCH // 2) as q:
                    onehots(2 * q, 0)
                    apply(2 * q - 1, 1)
                    onehots(2 * q + 1, 1)
                    apply(2 * q, 0)
                apply(GCH - 1, 1)

            def gated_lo(tiles):
                with dve.Fori(0, HT // 4) as q:
                    for k in range(4):
                        dve.wait_ge(g_hi_ready, 4 * q + (tiles + k + 1))
                        V.tensor_tensor(g_lo[:, k, :], hidden_tile(4 * q + k),
                                        g_hi[:, k, :].bitcast(F32), ALU.subtract).then_inc(g_lo_ready, 1)

            def add_acc(n_slabs, c0):
                dve.wait_ge(slab_used, n_slabs)
                for c in range(4):
                    V.tensor_tensor(x[:, c0 + c, :], ps[:, ACC + c, 0:T], x[:, c0 + c, :],
                                    ALU.add).then_inc(x_updated, 1)

            def add_projection(L):
                for n in range(OUT_N):
                    dve.wait_ge(slab_used, L * SLABS + OUT0 + n + 1)
                    bias = 0.0 if L == 0 else col("cf_b_pw2", n)
                    V.scalar_tensor_tensor(out=x[:, n, :], in0=ps[:, LIN + n % 2, 0:T], scalar=bias,
                                           in1=x[:, n, :], op0=ALU.add, op1=ALU.add).then_inc(x_updated, 1)

            def peer(L):
                base = L * SLABS
                use = L * USES
                squares(L * X_VD + X_MIX)
                normed(SUM_FFN[L], "norm_ffn", L * CH)
                publish(PUB_FFN[L])
                route(L)
                dve.wait_ge(picks_copied, 3 * L + 3)
                for b in range(2):
                    dve.wait_ge(evacuated[b], use + USE_MIX)
                expand_gates(2 * L, 0)
                gated_lo(256 * L)
                add_acc(base + MIX0, 0)
                gated_lo(256 * L + 64)
                add_acc(base + VC0 - 2, 4)
                for b in range(2):
                    dve.wait_ge(evacuated[b], use + USES)
                expand_gates(2 * L + 1, 1)
                gated_lo(256 * L + 128)
                add_acc(base + VD0, 0)
                gated_lo(256 * L + 192)
                add_acc(base + SLABS, 4)

            squares(0)
            did(V.memset(ext[:, :, 0:RG_W - 1], 0.0))
            state = col("state_conv", 0, 192).rearrange("p (c s k) -> p c s k", c=CH, s=NSEQ)
            for c in range(CH):
                did(V.tensor_copy(seqs(ext[:, c, EXT_S:EXT])[:, :, 0:RG_W - 1], state[:, c, :, :]))
            decay_columns()
            normed(SUM_MIX[0], "norm_mix", 0)
            publish(PUB_MIX[0])
            settle()
            rg_mixer()
            add_projection(0)
            peer(0)
            squares(X_VD)
            did(V.memset(z_ext[:, :, 0:CF_W - 1], 0.0))
            dve.wait_ge(loaded_l, 16 * 7)
            for c in range(CH):
                did(V.tensor_copy(seqs(z_ext[:, c, ZEXT_S:ZEXT])[:, :, 0:CF_W - 1], cstate[:, c, :, :]))
            normed(SUM_MIX[1], "norm_mix", CH)
            publish(PUB_MIX[1])
            settle()
            conformer()
            add_projection(1)
            peer(1)
            squares(DEPTH * X_VD)
            normed(SUM_FINAL, "norm_final", 0)


def _columns(v):
    return v.reshape(-1, CH, P).transpose(2, 0, 1).reshape(P, -1)


def _linear_slabs(w):
    return w.reshape(CH, P, -1, P).transpose(2, 1, 0, 3).reshape(-1, P, D)


def _layer_slabs(np, w_in, order, w_out, w_q, u, v):
    w_in = _linear_slabs(w_in)[order]
    u = u.reshape(P, P, CH, P).transpose(0, 3, 2, 1).reshape(2, HT, P, D)
    v = v.reshape(2, HT // 2, 2, P, 2, 512).transpose(0, 4, 1, 3, 2, 5).reshape(2, 2, HT // 2, P, D)
    mix = np.concatenate([v[0, 1][:, None], u[1].reshape(HT // 2, 2, P, D)], axis=1).reshape(-1, P, D)
    return [w_in, _linear_slabs(w_out), _linear_slabs(w_q), u[0], v[0, 0], mix, v[1, 0], v[1, 1]]


def kernel(**inputs):
    import numpy as _np
    import concourse.bacc as _bacc
    from concourse import mybir as _mybir
    from concourse.bass_utils import run_bass_kernel_spmd as _run

    a = {k: _np.asarray(v) for k, v in inputs.items()}
    first = list(range(CH))
    gate_last = [CH + c for c in first] + first
    by_pairs = [n for c in first for n in (CH + c, c)]
    slabs = []
    slabs += _layer_slabs(_np, a["rg_w_in"][0], gate_last, a["rg_w_out"][0], a["peer_w_q"][0],
                          a["peer_u"][0], a["peer_v"][0])
    slabs += _layer_slabs(_np, a["cf_w_pw1"][0], by_pairs, a["cf_w_pw2"][0], a["peer_w_q"][1],
                          a["peer_u"][1], a["peer_v"][1])
    x0 = _np.concatenate([a["x_prompt"].reshape(TP, D), a["x_sample"].reshape(TS, D)], axis=0)
    packed = []
    for name in ("norm_mix", "norm_ffn", "norm_final", "rg_conv_w", "rg_conv_b", "rg_b_a", "rg_b_i",
                 "rg_lambda", "cf_b_pw1", "cf_dw_w", "cf_dw_b", "cf_ln_g", "cf_ln_b", "cf_b_pw2"):
        packed.append(_columns(a[name]))
    packed.append(a["state_rglru_h"].reshape(NSEQ, CH, P).transpose(2, 1, 0).reshape(P, -1))
    packed.append(a["state_rglru_conv"].reshape(NSEQ, RG_W - 1, CH, P).transpose(3, 2, 0, 1).reshape(P, -1))
    gates = _np.stack([a["rg_w_a"][0], a["rg_w_i"][0]])
    arrays = {
        "x": x0.reshape(T, CH, P).transpose(2, 1, 0),
        "stream": _np.concatenate(slabs, axis=0),
        "cols": _np.concatenate(packed, axis=1),
        "keys": a["peer_sub_keys"].reshape(DEPTH, GROUPS, KEYS, P).transpose(0, 3, 1, 2),
        "blocks": gates.reshape(2, CH, 2, 64, 64).transpose(0, 2, 3, 1, 4),
        "cstate": a["state_conformer_conv"].reshape(NSEQ, CF_W - 1, CH, P).transpose(3, 2, 0, 1),
    }
    arrays = {k: _np.ascontiguousarray(v) for k, v in arrays.items()}

    nc = _bacc.Bacc("TRN2", target_bir_lowering=False, num_devices=1)
    f32 = _mybir.dt.float32
    args = [nc.dram_tensor(f"{k}_dram", v.shape, f32, kind="ExternalInput").ap() for k, v in arrays.items()]
    outs = {"y_t": (P, CH, T), "h_t": (P, CH, 1 + NSEQ), "rgc_t": (P, CH, 1 + NSEQ, RG_W - 1),
            "cfp_t": (P, CH, CF_W - 1), "cfs_t": (P, CH, NSEQ, CF_W - 1)}
    args += [nc.dram_tensor(f"{k}_dram", v, f32, kind="ExternalOutput").ap() for k, v in outs.items()]
    build(nc, *args)
    r = _run(nc, [{f"{k}_dram": v for k, v in arrays.items()}], core_ids=[0]).results[0]

    y = r["y_t_dram"].transpose(2, 1, 0).reshape(T, D)
    h = r["h_t_dram"].transpose(2, 1, 0).reshape(1 + NSEQ, D)
    rgc = r["rgc_t_dram"].transpose(2, 3, 1, 0).reshape(1 + NSEQ, RG_W - 1, D)
    cfp = r["cfp_t_dram"].transpose(2, 1, 0).reshape(1, 1, CF_W - 1, D)
    cfs = r["cfs_t_dram"].transpose(2, 3, 1, 0).reshape(1, NSEQ, CF_W - 1, D)
    return (y[:TP].reshape(1, TP, D), y[TP:].reshape(NSEQ, SL, D), h[None, :1], rgc[None, :1], cfp,
            h[None, 1:], rgc[None, 1:], cfs)
```

```python
from contextlib import ExitStack

import concourse.bass as bass
from concourse import mybir

ALU = mybir.AluOpType
ACT = mybir.ActivationFunctionType
AX_X = mybir.AxisListType.X
F32 = mybir.dt.float32
F32R = mybir.dt.float32r
BF16 = mybir.dt.bfloat16
U32 = mybir.dt.uint32

P = 128
D = 1024
CH = D // P
TP = 256
NSEQ, SL = 8, 4
TS = NSEQ * SL
T = TP + TS
RG_W, CF_W = 4, 31
SIDE_TAPS = 9
HEADS, KEYS, TOPK = 8, 128, 16
GROUPS = 2 * HEADS
PICKS = HEADS * TOPK
TT, NT = 96, 3
EPS = 1e-6
RG_C = 8.0
LOWEST = -3.0e38

SLOTS = 4
LEAD = 3
HT = 64
IN0, IN_N = 0, 16
OUT0, OUT_N = 16, 8
Q0, Q_N = 24, 16
UA0, UA_N = 40, HT
VA0, VA_N = 104, HT // 2
MIX0, MIX_N = 136, 96
VC0, VC_N = 232, HT // 2
VD0, VD_N = 264, HT // 2
SLABS = 296
DEPTH = 2
TOTAL = DEPTH * SLABS
USE_IN, USE_Q, USE_UA, USE_MIX, USES = 0, 8, 16, 48, 80
X_MIX, X_VA, X_VB, X_VC, X_VD = 8, 12, 16, 20, 24

SUM_MIX, SUM_FFN, SUM_MEAN, SUM_VAR, SUM_FINAL = (0, 2), (1, 5), 3, 4, 6
SQ_MIX, SQ_FFN, SQ_VAR, SQ_FINAL = (1, 3), (2, 5), 4, 6
SRC_MIX, SRC_LRU, SRC_FFN = (0, 3 * CH), CH, (2 * CH, 4 * CH + 3)
SRC_CONV, SRC_CENTRED, SRC_SCALED, SRC_FINAL = 4 * CH + 1, 4 * CH + 2, 4 * CH + 3, 5 * CH + 3
PUB_MIX, PUB_OUT, PUB_FFN = (0, 3), (1, 4), (2, 5)
ROUTE_STEPS = 16
CF_STORES = 1 + CH

GTOK = 8
GCH = T // GTOK
ACT_TOK = 6
GBUF = 4
GBANKS = (2, 3, 0, 1)
TERMS = 3

COLS, _n = {}, 0
for _name, _w in (("norm_mix", 16), ("norm_ffn", 16), ("norm_final", 8), ("rg_conv_w", 32),
                  ("rg_conv_b", 8), ("rg_b_a", 8), ("rg_b_i", 8), ("rg_lambda", 8),
                  ("cf_b_pw1", 16), ("cf_dw_w", CF_W * 8), ("cf_dw_b", 8), ("cf_ln_g", 8),
                  ("cf_ln_b", 8), ("cf_b_pw2", 8), ("state_h", 64), ("state_conv", 192)):
    COLS[_name] = _n
    _n += _w
NCOL = _n

EXT = TP + RG_W - 1 + NSEQ * (SL + RG_W - 1)
EXT_S = TP + RG_W - 1
ZEXT = TP + CF_W - 1 + NSEQ * (SL + CF_W - 1)
ZEXT_S = TP + CF_W - 1
ZROW = SL + CF_W - 1


def build(nc, x0, stream, cols_d, keys_d, blocks_d, cstate_d, y_d, h_d, rgc_d, cfp_d, cfs_d):
    with ExitStack() as ctx:
        def sb(name, shape, dt=F32):
            return ctx.enter_context(nc.sbuf_tensor(name, shape, dt))

        def sem(name):
            return ctx.enter_context(nc.semaphore(name))

        x = sb("x", [P, CH, T])
        act_hi = sb("act_hi", [P, CH, T], F32R)
        act_lo = sb("act_lo", [P, CH, T], F32R)
        land = sb("land", [P, SLOTS, D])
        w_hi = sb("w_hi", [P, SLOTS, D], F32R)
        w_lo = sb("w_lo", [P, SLOTS, D], F32R)
        hidden = sb("hidden", [P, HT, T])
        g_hi = sb("g_hi", [P, 4, T], F32R)
        g_lo = sb("g_lo", [P, 4, T], F32R)
        work = sb("work", [P, 8448])
        cols = sb("cols", [P, NCOL])
        decay = sb("decay", [P, 2, CH])
        iota = sb("iota", [P, KEYS])
        ident = sb("ident", [P, P])
        ones = sb("ones", [P, P])
        zeros = sb("zeros", [P, T], BF16)
        rstd = sb("rstd", [P, T])
        picks_tok = sb("picks_tok", [P, 3, NT, PICKS])
        picks = sb("picks", [P, 3, T])
        gate_terms = sb("gate_terms", [P, 2, T], BF16)
        head_sum = sb("head_sum", [P, NT * HEADS])
        held = sb("held", [P, 8 + ROUTE_STEPS + 1])
        h_last = sb("h_last", [P, CH, 1 + NSEQ])
        rg_last = sb("rg_last", [P, CH, 1 + NSEQ, RG_W - 1])

        flat = hidden[:, :, :].rearrange("p a t -> p (a t)")

        def view(base, lo, *dims):
            n = 1
            for d in dims:
                n *= d
            v = base[:, lo:lo + n]
            names = "abcd"[:len(dims)]
            if len(dims) > 1:
                v = v.rearrange(f"p ({' '.join(names)}) -> p {' '.join(names)}",
                                **dict(zip(names, dims)))
            return v

        def hidden_tile(slot):
            return hidden[:, bass.ds(slot, 1), :].rearrange("p o t -> p (o t)")

        CT = CH * T
        gate = view(flat, 0, CH, T)
        xc = view(flat, CT, CH, T)
        r_h = view(flat, 2 * CT, CH, T)
        i_g = view(flat, 3 * CT, CH, T)
        a_g = view(flat, 4 * CT, CH, T)
        u_g = view(flat, 5 * CT, CH, T)
        ext = view(flat, 6 * CT, CH, EXT)
        z_ext = view(flat, 0, CH, ZEXT)
        cv = view(flat, CH * ZEXT, CH, T)
        sq_cf = view(flat, CH * ZEXT + CT, CH, T)
        glu_gate = view(flat, CH * ZEXT + 2 * CT, 2, T)
        mean = view(flat, CH * ZEXT + 2 * CT + 2 * T, T)
        q_t = view(flat, 0, GROUPS, T)
        SCORES = HT * T - NT * GROUPS * KEYS
        scores = view(flat, SCORES, NT, GROUPS * KEYS)
        U_CLEAR = SCORES // T // SLOTS
        A, B, C, E = 0, 2304, 4352, 6400
        work_f = work[:, :]
        sq = view(work_f, A, CH, T)
        keys = view(work_f, B, GROUPS, KEYS)
        blocks = view(work_f, C, 2, CH, P)
        cstate = view(work_f, C, CH, NSEQ, CF_W - 1)
        conv_prod = view(work_f, E, NSEQ, SL, CF_W)
        tap_prod = view(work_f, A, SIDE_TAPS, TP)
        cv_odd = view(work_f, C, TP)
        cv_pool = view(work_f, C + TP, 2, TP)
        s_tile = view(work_f, A, GROUPS, KEYS)
        s_rest = view(work_f, C, GROUPS, KEYS)
        top_v = view(work_f, B, GROUPS, TOPK)
        top_i = view(work_f, B + 256, GROUPS, TOPK).bitcast(U32)
        top_f = view(work_f, B + 512, GROUPS, TOPK)
        best = view(work_f, B + 768, HEADS, TOPK)
        pos = view(work_f, B + 896, HEADS, TOPK).bitcast(U32)
        pos_ab = view(work_f, B + 1024, 2, PICKS).bitcast(U32)
        pos_f = view(work_f, B + 1280, 2, PICKS)
        cand = view(work_f, E, HEADS, TOPK * TOPK)
        cand_rest = view(work_f, A, HEADS, TOPK * TOPK)
        hot = [view(work_f, off, HEADS, TOPK, TOPK) for off in (E, C)]
        work_b = work[:, :].bitcast(BF16)
        onehot_j = view(work_b, 0, GBUF, GTOK // 2, KEYS * 2)
        mask_i = view(work_b, GBUF * GTOK * KEYS, GBUF, GTOK // 2, HT * 2)
        onehot_i = [view(work_b, GBUF * GTOK * (KEYS + (k + 1) * HT), GBUF, GTOK // 2, HT * 2)
                    for k in range(TERMS)]
        ONEHOTS = GBUF * GTOK * (KEYS + (TERMS + 1) * HT)
        iota_rep = view(work_b, ONEHOTS, KEYS, 2)
        picks_b = view(work_b, ONEHOTS + KEYS * 2, 2, T)

        def hold(engine, k=0):
            if engine.engine == nc.scalar.engine:
                nc.scalar.copy(held[0:1, k:k + 1], ones[0:1, 0:1])
            else:
                nc.vector.tensor_copy(held[0:1, 8 + k:9 + k], ones[0:1, 0:1])

        ps = ctx.enter_context(nc.psum_tensor("ps", [P, 8, 512], F32))
        LIN, NORM, ACC = 0, 2, 4

        landed = [sem(f"landed_{k}") for k in range(SLOTS)]
        w_hi_ready = sem("w_hi_ready")
        w_lo_ready = sem("w_lo_ready")
        slab_used = sem("slab_used")
        evacuated = [sem("evacuated_0"), sem("evacuated_1")]
        loaded = sem("loaded")
        loaded_l = sem("loaded_l")
        consts_ready = sem("consts_ready")
        x_updated = sem("x_updated")
        sq_act = sem("sq_act")
        sq_dve = sem("sq_dve")
        summed = sem("summed")
        std_ready = sem("std_ready")
        src_ready = sem("src_ready")
        silu_ready = sem("silu_ready")
        act_hi_ready = sem("act_hi_ready")
        act_lo_ready = sem("act_lo_ready")
        conv_done = sem("conv_done")
        block_done = sem("block_done")
        block_read = sem("block_read")
        decay_exp = sem("decay_exp")
        decay_ready = sem("decay_ready")
        lru_act = sem("lru_act")
        lru_dve = sem("lru_dve")
        scored = sem("scored")
        scores_copied = sem("scores_copied")
        tile_staged = sem("tile_staged")
        exp_ready = sem("exp_ready")
        picks_ready = sem("picks_ready")
        picks_turned = sem("picks_turned")
        picks_copied = sem("picks_copied")
        masks_ready = sem("masks_ready")
        js_ready = sem("js_ready")
        firsts_ready = sem("firsts_ready")
        seconds_ready = sem("seconds_ready")
        thirds_ready = sem("thirds_ready")
        tails_ready = sem("tails_ready")
        expanded = sem("expanded")
        gated = sem("gated")
        g_hi_ready = sem("g_hi_ready")
        g_lo_ready = sem("g_lo_ready")
        step = sem("step")
        route_step = sem("route_step")
        glu_ready = sem("glu_ready")
        tap_product = sem("tap_product")
        taps_summed = sem("taps_summed")
        pool_sum_read = sem("pool_sum_read")
        stored = sem("stored")
        states_ready = sem("states_ready")
        states_out = sem("states_out")

        block = ctx.enter_context(nc.Block())

        def pairs(v):
            return v.rearrange("p a (n two) -> p a n two", two=2)

        def per_token(v, shape):
            return v.rearrange("p (a two) -> p a two", two=2).unsqueeze(2).to_broadcast(shape)

        def of_token(v, buf, t):
            return v[:, buf, t // 2, :].rearrange("p (n two) -> p n two", two=2)[:, :, t % 2]

        def col(name, c, n=1):
            return cols[:, COLS[name] + c:COLS[name] + c + n]

        @block.sync
        def _(sp):
            sp.dma_start(x[:, :, :], x0).then_inc(loaded, 16)
            sp.dma_start(cols[:, :], cols_d).then_inc(loaded, 16)
            for k in range(SLOTS):
                sp.dma_start(land[:, k, :], stream[k]).then_inc(landed[k], 16)
            with sp.Fori(1, TOTAL // SLOTS) as q:
                for k in range(SLOTS):
                    sp.wait_ge(w_lo_ready, 4 * q + (k - 3))
                    sp.dma_start(land[:, k, :], stream[4 * q + k]).then_inc(landed[k], 16)
            for c in range(CH):
                sp.wait_ge(src_ready, SRC_FINAL + c + 1)
                sp.dma_start(y_d[:, c, :], sq[:, c, :]).then_inc(stored, 16)
            sp.wait_ge(stored, 16 * (CH + CF_STORES))
            sp.wait_ge(states_out, 32)

        @block.gpsimd
        def _(pool):
            nc.gpsimd.memset(ones[:, :], 1.0).then_inc(consts_ready, 1)
            nc.gpsimd.memset(zeros[:, :], 0.0).then_inc(consts_ready, 1)
            nc.gpsimd.memset(ident[:, :], 0.0).then_inc(consts_ready, 1)
            nc.gpsimd.memset(blocks, 0.0).then_inc(consts_ready, 1)
            nc.gpsimd.iota(iota[:, :], pattern=[[1, KEYS]], base=0, channel_multiplier=0,
                           allow_small_or_imprecise_dtypes=True).then_inc(consts_ready, 1)
            pool.wait_ge(consts_ready, 5)
            nc.gpsimd.affine_select(out=ident[:, :], in_=ident[:, :], compare_op=ALU.not_equal,
                                    fill=1.0, base=0, pattern=[[-1, P]],
                                    channel_multiplier=1).then_inc(consts_ready, 1)
            def split_slabs(first, end):
                with pool.Fori(first // SLOTS, end // SLOTS) as q:
                    for k in range(SLOTS):
                        pool.wait_ge(w_hi_ready, 4 * q + (k + 1))
                        nc.gpsimd.tensor_tensor(w_lo[:, k, :], land[:, k, :], w_hi[:, k, :].bitcast(F32),
                                                ALU.subtract).then_inc(w_lo_ready, 1)

            def weight_onehots(half_index):
                first = GCH * half_index
                with pool.Fori(0, GCH // GBUF) as q:
                    for buf in range(GBUF):
                        pool.wait_ge(masks_ready, GBUF * q + (first + buf + 1))
                        tok = bass.ds((GBUF * q + buf) * GTOK, GTOK)
                        shape = [P, GTOK // 2, HT, 2]
                        nc.gpsimd.tensor_tensor(
                            pairs(onehot_i[0][:, buf, :, :]), pairs(mask_i[:, buf, :, :]),
                            per_token(gate_terms[:, 0, tok], shape), ALU.mult).then_inc(firsts_ready, 1)
                        left = (GTOK - ACT_TOK) // 2
                        tok = bass.ds((GBUF * q + buf) * GTOK + ACT_TOK, GTOK - ACT_TOK)
                        nc.gpsimd.tensor_tensor(
                            pairs(onehot_i[2][:, buf, ACT_TOK // 2:, :]),
                            pairs(mask_i[:, buf, ACT_TOK // 2:, :]),
                            per_token(picks[:, 2, tok], [P, left, HT, 2]), ALU.mult).then_inc(tails_ready, 1)

            def conformer_taps():
                def split_slab(n):
                    pool.wait_ge(w_hi_ready, n + 1)
                    k = n % SLOTS
                    nc.gpsimd.tensor_tensor(w_lo[:, k, :], land[:, k, :], w_hi[:, k, :].bitcast(F32),
                                            ALU.subtract).then_inc(w_lo_ready, 1)

                for n in range(2):
                    split_slab(SLABS + n)
                for c in range(CH):
                    for n in range(2 * c + 2, 2 * c + 4):
                        split_slab(SLABS + n)
                    if c >= 2:
                        pool.wait_ge(pool_sum_read, c - 1)
                    dst = cv_pool[:, c % 2, :]
                    for k in range(1, SIDE_TAPS):
                        pool.wait_ge(tap_product, SIDE_TAPS * c + k + 1)
                        if k > 1:
                            pool.wait_ge(taps_summed, (SIDE_TAPS - 1) * c + k - 1)
                        nc.gpsimd.tensor_tensor(dst, dst if k > 1 else tap_prod[:, 0, :], tap_prod[:, k, :],
                                                ALU.add).then_inc(taps_summed, 1)
                for n in range(2 * CH + 2, 2 * CH + SLOTS):
                    split_slab(SLABS + n)

            done = 0
            for L in range(DEPTH):
                if L == 1:
                    split_slabs(done, SLABS)
                    conformer_taps()
                    done = SLABS + 2 * CH + SLOTS
                for half, start in enumerate((VA0, VC0)):
                    split_slabs(done, L * SLABS + start)
                    done = L * SLABS + start
                    weight_onehots(2 * L + half)
            split_slabs(done, TOTAL)

        @block.scalar
        def _(act):
            def side_products(c):
                act.wait_ge(glu_ready, c + 1)
                for k in range(SIDE_TAPS):
                    if c:
                        act.wait_ge(taps_summed, (SIDE_TAPS - 1) * (c - 1) + max(k, 1))
                    nc.scalar.activation(tap_prod[:, k, :], z_ext[:, c, k:k + TP], ACT.Copy,
                                         scale=col("cf_dw_w", k * CH + c)).then_inc(tap_product, 1)

            def split(q, m):
                q, m = q + m // SLOTS, m % SLOTS
                first = isinstance(q, int) and q == 0
                act.wait_ge(landed[m], 16 * q + 16)
                if not first:
                    act.wait_ge(slab_used, 4 * q + (m - 3))
                nc.scalar.copy(w_hi[:, m, :], land[:, m, :]).then_inc(w_hi_ready, 1)

            def split_ahead(q, m):
                if isinstance(q, int) and 4 * q + m + LEAD >= TOTAL:
                    return
                split(q, m + LEAD)

            def squares(x_count):
                if x_count:
                    act.wait_ge(x_updated, x_count)
                else:
                    act.wait_ge(loaded, 32)
                nc.scalar.activation(sq[:, 0:4, :], x[:, 0:4, :], ACT.Square).then_inc(sq_act, 1)

            def root(n):
                act.wait_ge(summed, n + 1)
                nc.scalar.activation(rstd[:, :], ps[:, NORM, 0:T], ACT.Sqrt, bias=EPS,
                                     scale=1.0 / D).then_inc(std_ready, 1)

            def publish(ready, base):
                for c in range(CH):
                    act.wait_ge(ready, base + c + 1)
                    nc.scalar.copy(act_hi[:, c, :], sq[:, c, :]).then_inc(act_hi_ready, 1)

            def third_terms(half_index):
                first = GCH * half_index
                with act.Fori(0, GCH // GBUF) as q:
                    for buf in range(GBUF):
                        act.wait_ge(masks_ready, GBUF * q + (first + buf + 1))
                        for t in range(ACT_TOK):
                            token = bass.ds((GBUF * q + buf) * GTOK + t, 1)
                            ins = nc.scalar.activation(of_token(onehot_i[2], buf, t), of_token(mask_i, buf, t),
                                                       ACT.Copy, scale=picks[:, 2, token])
                        ins.then_inc(thirds_ready, 1)

            def gated_hi(slot, ring):
                nc.scalar.copy(g_hi[:, ring, :], hidden_tile(slot)).then_inc(g_hi_ready, 1)

            def layer(L):
                base = L * SLABS
                use = L * USES

                def lin_done(n):
                    act.wait_ge(slab_used, base + n + 1)

                squares(L * X_VD)
                root(SUM_MIX[L])
                publish(src_ready, SRC_MIX[L])
                if L == 0:
                    for n in range(IN_N):
                        split_ahead(base // 4, IN0 + n)
                        lin_done(IN0 + n)
                        c = n % CH
                        if n < CH:
                            nc.scalar.copy(ext[:, c, RG_W - 1:EXT_S], ps[:, LIN + n % 2, 0:TP])
                            nc.scalar.copy(
                                ext[:, c, EXT_S:EXT].rearrange("p (s w) -> p s w", s=NSEQ)[:, :, RG_W - 1:],
                                ps[:, LIN + n % 2, TP:T].rearrange("p (s w) -> p s w", s=NSEQ),
                            ).then_inc(evacuated[n % 2], 1)
                        else:
                            nc.scalar.activation(gate[:, c, :], ps[:, LIN + n % 2, 0:T],
                                                 ACT.Gelu_apprx_tanh).then_inc(evacuated[n % 2], 1)
                    for c in range(CH):
                        for m, (dst, bias) in enumerate(((r_h, "rg_b_a"), (i_g, "rg_b_i"))):
                            act.wait_ge(block_done, 2 * c + m + 1)
                            nc.scalar.activation(dst[:, c, :], ps[:, NORM + m, 0:T], ACT.Sigmoid,
                                                 bias=col(bias, c)).then_inc(block_read, 1)
                    act.wait_ge(decay_ready, 1)
                    act.wait_ge(block_read, 2 * CH)
                    for c in range(CH):
                        nc.scalar.activation(a_g[:, c, :], r_h[:, c, :], ACT.Exp,
                                             scale=decay[:, 0, c:c + 1]).then_inc(lru_act, 1)
                        nc.scalar.activation(u_g[:, c, :], r_h[:, c, :], ACT.Tanh,
                                             scale=decay[:, 1, c:c + 1]).then_inc(lru_act, 1)
                    for half in range(2):
                        act.wait_ge(lru_dve, half + 1)
                        part = u_g[:, 4 * half:4 * half + 4, :]
                        nc.scalar.activation(part, part, ACT.Sqrt).then_inc(lru_act, 1)
                    publish(src_ready, SRC_LRU)
                else:
                    for n in range(IN_N):
                        split_ahead(base // 4, IN0 + n)
                        if n % 2:
                            side_products(n // 2)
                            continue
                        lin_done(IN0 + n)
                        c = n // 2
                        if c >= 2:
                            act.wait_ge(evacuated[1], use + USE_IN + c - 1)
                        nc.scalar.activation(glu_gate[:, c % 2, :], ps[:, LIN, 0:T], ACT.Sigmoid,
                                             bias=col("cf_b_pw1", CH + c)).then_inc(evacuated[0], 1)
                    act.wait_ge(evacuated[1], use + USE_Q)
                    act.dma_start(cfp_d, z_ext[:, :, ZEXT_S - (CF_W - 1):ZEXT_S]).then_inc(stored, 16)
                    for c in range(CH):
                        act.dma_start(cfs_d[:, c], z_ext[:, c, ZEXT_S:ZEXT].rearrange(
                            "p (s w) -> p s w", s=NSEQ)[:, :, SL:]).then_inc(stored, 16)
                    act.wait_ge(summed, SUM_MEAN + 1)
                    nc.scalar.activation(mean, ps[:, NORM, 0:T], ACT.Copy,
                                         scale=1.0 / D).then_inc(std_ready, 1)
                    act.wait_ge(src_ready, SRC_CENTRED)
                    nc.scalar.activation(sq_cf[:, 0:4, :], cv[:, 0:4, :], ACT.Square).then_inc(sq_act, 1)
                    root(SUM_VAR)
                    act.wait_ge(src_ready, SRC_SCALED)
                    for c in range(CH):
                        nc.scalar.activation(sq[:, c, :], cv[:, c, :], ACT.Silu,
                                             bias=col("cf_ln_b", c),
                                             scale=col("cf_ln_g", c)).then_inc(silu_ready, 1)
                    publish(silu_ready, 0)
                for n in range(OUT_N):
                    split_ahead(base // 4, OUT0 + n)
                if L == 0:
                    act.wait_ge(states_ready, 3 + CH)
                    act.dma_start(h_d, h_last[:, :, :]).then_inc(states_out, 16)
                    act.dma_start(rgc_d, rg_last[:, :, :, :]).then_inc(states_out, 16)
                squares(L * X_VD + X_MIX)
                root(SUM_FFN[L])
                publish(src_ready, SRC_FFN[L])
                if L == 1:
                    act.wait_ge(stored, 16 * CF_STORES)
                for n in range(Q_N):
                    split_ahead(base // 4, Q0 + n)
                    lin_done(Q0 + n)
                    nc.scalar.copy(q_t[:, n, :], ps[:, LIN + n % 2, 0:T]).then_inc(evacuated[n % 2], 1)

                def u_tile(slot, bank):
                    nc.scalar.activation(hidden_tile(slot), ps[:, bank, 0:T],
                                         ACT.Gelu_apprx_tanh).then_inc(evacuated[bank], 1)

                def u_steps(q):
                    for k in range(4):
                        split_ahead(base // 4 + UA0 // 4 + q, k)
                        act.wait_ge(slab_used, 4 * q + (base + UA0 + k + 1))
                        hold(act, k)
                        u_tile(4 * q + k, k % 2)

                with act.Fori(0, U_CLEAR) as q:
                    u_steps(q)
                act.wait_ge(tile_staged, NT * (L + 1))
                with act.Fori(U_CLEAR, HT // 4) as q:
                    u_steps(q)

                act.wait_ge(route_step, ROUTE_STEPS * NT * (L + 1))
                nc.scalar.activation(picks_tok[0:TT, 2, :, :], picks_tok[0:TT, 2, :, :],
                                     ACT.Exp).then_inc(exp_ready, 1)
                for kind in range(3):
                    act.wait_ge(picks_turned, 3 * L + kind + 1)
                    nc.scalar.copy(picks[:, kind, :], ps[:, ACC + kind, 0:T]).then_inc(picks_copied, 1)
                third_terms(2 * L)

                def v_steps(start, q):
                    for k in range(4):
                        act.wait_ge(slab_used, 4 * q + (base + start + k - 1))
                        for ii in range(2):
                            gated_hi(8 * q + (2 * k + ii), (2 * k + ii) % 4)
                        split_ahead(base // 4 + start // 4 + q, k)

                act.wait_ge(gated, GCH * (2 * L + 1))
                with act.Fori(0, VA_N // 4) as q:
                    v_steps(VA0, q)

                def mix_steps(q, last):
                    for k in range(4):
                        m = 3 * k
                        Q = base // 4 + MIX0 // 4 + 3 * q
                        split_ahead(Q, m)
                        split_ahead(Q, m + 1)
                        if not (last and k == 3):
                            for ii in range(2):
                                gated_hi(8 * q + (2 * k + 2 + ii), (2 * k + 2 + ii) % 4)
                        for r in range(2):
                            if r:
                                split_ahead(Q, m + 2)
                            act.wait_ge(slab_used, 12 * q + (base + MIX0 + m + r + 2))
                            hold(act, 2 * k + r)
                            u_tile(8 * q + (2 * k + r), r)

                act.wait_ge(slab_used, base + MIX0 - 1)
                for ii in range(2):
                    gated_hi(ii, ii)
                with act.Fori(0, MIX_N // 12 - 1) as q:
                    mix_steps(q, False)
                mix_steps(MIX_N // 12 - 1, True)

                third_terms(2 * L + 1)
                act.wait_ge(gated, GCH * (2 * L + 2))
                for start in (VC0, VD0):
                    if L == DEPTH - 1 and start == VD0:
                        with act.Fori(0, VD_N // 4 - 1) as q:
                            v_steps(start, q)
                        v_steps(start, VD_N // 4 - 1)
                    else:
                        with act.Fori(0, VD_N // 4) as q:
                            v_steps(start, q)

            act.wait_ge(consts_ready, 4)
            act.dma_start(keys, keys_d[0]).then_inc(loaded_l, 16)
            for m in range(2):
                for b in range(2):
                    act.dma_start(blocks[64 * b:64 * b + 64, m, :, 64 * b:64 * b + 64],
                                  blocks_d[m, b]).then_inc(loaded_l, 16)
            for m in range(LEAD):
                split(0, m)
            act.wait_ge(decay_exp, 1)
            nc.scalar.activation(decay[:, 1, :], decay[:, 0, :], ACT.Exp).then_inc(decay_exp, 1)
            layer(0)
            act.dma_start(keys, keys_d[1]).then_inc(loaded_l, 16)
            act.dma_start(cstate, cstate_d).then_inc(loaded_l, 16)
            layer(1)
            squares(DEPTH * X_VD)
            root(SUM_FINAL)

        @block.tensor
        def _(pe):
            def column_sum(n, src, waits):
                for s, v in waits:
                    pe.wait_ge(s, v)
                for c in range(CH):
                    mm = nc.tensor.matmul(ps[:, NORM, 0:T], ones[:, :], src[:, c, :],
                                          start=(c == 0), stop=(c == CH - 1))
                mm.then_inc(summed, 1)

            def three_terms(out, wsl, slot, hi, lo, start, stop, **kw):
                nc.tensor.matmul(out, w_hi[:, slot, wsl], hi, start=start, stop=False, **kw)
                nc.tensor.matmul(out, w_lo[:, slot, wsl], hi, start=False, stop=False, **kw)
                return nc.tensor.matmul(out, w_hi[:, slot, wsl], lo, start=False, stop=stop, **kw)

            def linear(q, m, bank, read, count, published=None):
                q, m = q + m // SLOTS, m % SLOTS
                pe.wait_ge(w_lo_ready, 4 * q + (m + 1))
                if not (isinstance(count, int) and count == 0):
                    pe.wait_ge(read, count)
                for c in range(CH):
                    if published is not None:
                        pe.wait_ge(act_lo_ready, published * CH + c + 1)
                    mm = three_terms(ps[:, LIN + bank, 0:T], slice(c * P, c * P + P), m,
                                     act_hi[:, c, :], act_lo[:, c, :], c == 0, c == CH - 1)
                mm.then_inc(slab_used, 1)

            def v_slab(q, m, ring, tiles):
                q, m = q + m // SLOTS, m % SLOTS
                pe.wait_ge(w_lo_ready, 4 * q + (m + 1))
                for ii in range(2):
                    pe.wait_ge(g_lo_ready, tiles + (ii + 1))
                    for c in range(4):
                        mm = three_terms(ps[:, ACC + c, 0:T], slice(ii * 512 + c * P, ii * 512 + c * P + P), m,
                                         g_hi[:, ring + ii, :], g_lo[:, ring + ii, :], False, False,
                                         skip_group_check=True)
                mm.then_inc(slab_used, 1)

            def clear_acc(x_count):
                for c in range(4):
                    pe.wait_ge(x_updated, x_count + (c - 3))
                    nc.tensor.matmul(ps[:, ACC + c, 0:T], zeros[:, 0:P], zeros[:, :], start=True,
                                     stop=False, skip_group_check=True)

            def expand_gates(half_index):
                first = GCH * half_index

                def chunk(g, buf, head):
                    pe.wait_ge(js_ready, g + (first + 1))
                    pe.wait_ge(firsts_ready, g + (first + 1))
                    pe.wait_ge(seconds_ready, g + (first + 1))
                    pe.wait_ge(thirds_ready, g + (first + 1))
                    pe.wait_ge(tails_ready, g + (first + 1))
                    if not head:
                        pe.wait_ge(gated, g + (first + 1 - GBUF))
                    for t in range(GTOK):
                        out = ps[:, GBANKS[buf], t * HT:(t + 1) * HT]
                        for k in range(TERMS):
                            mm = nc.tensor.matmul(out, of_token(onehot_j, buf, t), of_token(onehot_i[k], buf, t),
                                                  start=(k == 0), stop=(k == TERMS - 1))
                    mm.then_inc(expanded, 1)

                for b in range(2):
                    pe.wait_ge(evacuated[b], (half_index // 2) * USES + (USE_MIX, USES)[half_index % 2])
                for buf in range(GBUF):
                    chunk(buf, buf, True)
                with pe.Fori(1, GCH // GBUF) as q:
                    for buf in range(GBUF):
                        chunk(GBUF * q + buf, buf, False)

            def layer(L):
                base = L * SLABS
                use = L * USES
                q0 = base // 4
                column_sum(SUM_MIX[L], sq, ((sq_act, SQ_MIX[L]), (sq_dve, SQ_MIX[L])))
                for n in range(IN_N):
                    linear(q0, IN0 + n, n % 2, evacuated[n % 2], use + USE_IN + n // 2,
                           PUB_MIX[L] if n == 0 else None)
                if L == 0:
                    pe.wait_ge(loaded_l, 16 * 5)
                    for c in range(CH):
                        pe.wait_ge(conv_done, c + 1)
                        for m in range(2):
                            if c:
                                pe.wait_ge(block_read, 2 * c + m - 1)
                            nc.tensor.matmul(ps[:, NORM + m, 0:T], blocks[:, m, c, :], xc[:, c, :],
                                             start=True, stop=True).then_inc(block_done, 1)
                else:
                    column_sum(SUM_MEAN, cv, ((src_ready, SRC_CONV),))
                    column_sum(SUM_VAR, sq_cf, ((sq_act, SQ_VAR), (sq_dve, SQ_VAR)))
                for n in range(OUT_N):
                    if n < 2:
                        linear(q0, OUT0 + n, n, evacuated[n], use + USE_Q, PUB_OUT[L] if n == 0 else None)
                    else:
                        linear(q0, OUT0 + n, n % 2, x_updated, L * X_VD + n - 1)
                column_sum(SUM_FFN[L], sq, ((sq_act, SQ_FFN[L]), (sq_dve, SQ_FFN[L])))
                pe.wait_ge(x_updated, L * X_VD + X_MIX)
                for n in range(Q_N):
                    linear(q0, Q0 + n, n % 2, evacuated[n % 2], use + USE_Q + n // 2,
                           PUB_FFN[L] if n == 0 else None)
                pe.wait_ge(evacuated[0], use + USE_UA)
                pe.wait_ge(evacuated[1], use + USE_UA)
                pe.wait_ge(loaded_l, 16 * (5, 7)[L])
                for u in range(4 * NT):
                    tile, b = u // 4, u % 4
                    if u >= 6:
                        pe.wait_ge(scores_copied, 4 * NT * L + u - 5)
                    for g in range(4):
                        mm = nc.tensor.matmul(ps[0:TT, 2 + u % 6, g * KEYS:(g + 1) * KEYS],
                                              q_t[:, 4 * b + g, tile * TT:(tile + 1) * TT],
                                              keys[:, 4 * b + g, :], start=True, stop=True)
                    mm.then_inc(scored, 1)
                with pe.Fori(0, UA_N // 4) as q:
                    for k in range(4):
                        linear(q0 + UA0 // 4 + q, k, k % 2, evacuated[k % 2], 2 * q + (use + USE_UA + k // 2))
                pe.wait_ge(scores_copied, 4 * NT * (L + 1))
                for kind in range(3):
                    pe.wait_ge(picks_ready, L + 1)
                    for tile in range(NT):
                        mm = nc.tensor.transpose(ps[:, ACC + kind, tile * TT:(tile + 1) * TT],
                                                 picks_tok[0:TT, kind, tile, :], ident[0:TT, 0:TT])
                    mm.then_inc(picks_turned, 1)
                expand_gates(2 * L)
                pe.wait_ge(picks_copied, 3 * L + 3)
                clear_acc(L * X_VD + X_MIX)
                with pe.Fori(0, VA_N // 4) as q:
                    for k in range(4):
                        v_slab(q0 + VA0 // 4 + q, k, 2 * (k % 2), 8 * q + (256 * L + 2 * k))
                clear_acc(L * X_VD + X_VA)
                with pe.Fori(0, MIX_N // 12) as q:
                    for k in range(4):
                        Q = q0 + MIX0 // 4 + 3 * q
                        v_slab(Q, 3 * k, 2 * (k % 2), 8 * q + (256 * L + 64 + 2 * k))
                        for r in range(2):
                            linear(Q, 3 * k + 1 + r, r, evacuated[r], 4 * q + (use + USE_MIX + k))
                expand_gates(2 * L + 1)
                for n, start in enumerate((VC0, VD0)):
                    clear_acc(L * X_VD + (X_VB, X_VC)[n])
                    with pe.Fori(0, VC_N // 4) as q:
                        for k in range(4):
                            v_slab(q0 + start // 4 + q, k, 2 * (k % 2),
                                   8 * q + (256 * L + 128 + 64 * n + 2 * k))

            pe.wait_ge(consts_ready, 6)
            layer(0)
            layer(1)
            column_sum(SUM_FINAL, sq, ((sq_act, SQ_FINAL), (sq_dve, SQ_FINAL)))

        @block.vector
        def _(dve):
            steps = [0]
            V = nc.vector

            def did(ins):
                steps[0] += 1
                ins.then_inc(step, 1)

            def settle():
                dve.wait_ge(step, steps[0])

            def squares(x_count):
                if x_count:
                    dve.wait_ge(x_updated, x_count)
                else:
                    dve.wait_ge(loaded, 32)
                V.tensor_tensor(sq[:, 4:8, :], x[:, 4:8, :], x[:, 4:8, :], ALU.mult).then_inc(sq_dve, 1)

            def invert(n):
                dve.wait_ge(std_ready, n + 1)
                did(V.reciprocal(rstd[:, :], rstd[:, :]))
                settle()

            def normed(n, name, c0):
                invert(n)
                for c in range(CH):
                    V.scalar_tensor_tensor(out=sq[:, c, :], in0=x[:, c, :], scalar=col(name, c0 + c),
                                           in1=rstd[:, :], op0=ALU.mult,
                                           op1=ALU.mult).then_inc(src_ready, 1)

            def publish(n):
                for c in range(CH):
                    dve.wait_ge(act_hi_ready, n * CH + c + 1)
                    V.tensor_tensor(act_lo[:, c, :], sq[:, c, :], act_hi[:, c, :].bitcast(F32),
                                    ALU.subtract).then_inc(act_lo_ready, 1)

            def decay_columns():
                lam, s, e = col("rg_lambda", 0, CH), decay[:, 0, :], decay[:, 1, :]
                t = [view(work_f, E + CH * k, CH) for k in range(5)]
                did(V.tensor_scalar(t[0], lam, -1.0, None, ALU.mult))
                settle()
                did(V.tensor_tensor(t[1], lam, t[0], ALU.max))
                settle()
                V.tensor_scalar(s, t[1], -1.0, None, ALU.mult).then_inc(decay_exp, 1)
                dve.wait_ge(decay_exp, 2)
                did(V.tensor_scalar(t[1], e, 2.0, None, ALU.add))
                settle()
                did(V.reciprocal(t[2], t[1]))
                settle()
                did(V.tensor_tensor(t[1], e, t[2], ALU.mult))
                settle()
                did(V.tensor_tensor(t[2], t[1], t[1], ALU.mult))
                did(V.memset(t[3], 1.0 / 19))
                settle()
                for odd in range(17, 0, -2):
                    did(V.tensor_tensor(t[4], t[3], t[2], ALU.mult))
                    settle()
                    did(V.tensor_scalar(t[3], t[4], 1.0 / odd, None, ALU.add))
                    settle()
                did(V.tensor_tensor(t[4], t[3], t[1], ALU.mult))
                did(V.tensor_scalar(t[2], t[0], 0.0, None, ALU.max))
                settle()
                did(V.scalar_tensor_tensor(out=t[3], in0=t[4], scalar=2.0, in1=t[2],
                                           op0=ALU.mult, op1=ALU.add))
                settle()
                did(V.tensor_scalar(decay[:, 0, :], t[3], -RG_C, None, ALU.mult))
                V.tensor_scalar(decay[:, 1, :], t[3], RG_C, None, ALU.mult).then_inc(decay_ready, 1)

            def seqs(v):
                return v.rearrange("p (s w) -> p s w", s=NSEQ)

            def rg_mixer():
                for c in range(CH):
                    dve.wait_ge(evacuated[c % 2], USE_IN + c // 2 + 1)
                    for k in range(RG_W):
                        w = col("rg_conv_w", k * CH + c)
                        pairs = ((xc[:, c, 0:TP], ext[:, c, k:k + TP]),
                                 (seqs(xc[:, c, TP:T]), seqs(ext[:, c, EXT_S:EXT])[:, :, k:k + SL]))
                        for n, (dst, src) in enumerate(pairs):
                            if k == 0:
                                ins = V.tensor_scalar(dst, src, w, col("rg_conv_b", c), ALU.mult, ALU.add)
                            else:
                                ins = V.scalar_tensor_tensor(out=dst, in0=src, scalar=w, in1=dst,
                                                             op0=ALU.mult, op1=ALU.add)
                            if k == RG_W - 1 and n == 1:
                                ins.then_inc(conv_done, 1)
                            else:
                                did(ins)
                        if k < RG_W - 1:
                            settle()
                V.tensor_copy(rg_last[:, :, 0, :], ext[:, :, TP:EXT_S]).then_inc(states_ready, 1)
                for c in range(CH):
                    V.tensor_copy(rg_last[:, c, 1:, :],
                                  seqs(ext[:, c, EXT_S:EXT])[:, :, SL:]).then_inc(states_ready, 1)
                dve.wait_ge(conv_done, CH)
                for c in range(CH):
                    dve.wait_ge(block_read, 2 * c + 2)
                    did(V.tensor_tensor(i_g[:, c, :], i_g[:, c, :], xc[:, c, :], ALU.mult))
                tmp = r_h
                for half in range(2):
                    h4 = slice(4 * half, 4 * half + 4)
                    dve.wait_ge(lru_act, 2 * CH)
                    did(V.tensor_tensor(tmp[:, h4, :], a_g[:, h4, :], a_g[:, h4, :], ALU.mult))
                    settle()
                    V.scalar_tensor_tensor(out=u_g[:, h4, :], in0=tmp[:, h4, :], scalar=1.0,
                                           in1=u_g[:, h4, :], op0=ALU.add,
                                           op1=ALU.mult).then_inc(lru_dve, 1)
                h0 = col("state_h", 0, 64).rearrange("p (c s) -> p c s", c=CH)
                carry = view(work_f, E, CH, NSEQ)
                a_first = a_g[:, :, TP:T].rearrange("p c (s w) -> p c s w", s=NSEQ)[:, :, :, 0]
                u_first = u_g[:, :, TP:T].rearrange("p c (s w) -> p c s w", s=NSEQ)[:, :, :, 0]
                for half in range(2):
                    h4 = slice(4 * half, 4 * half + 4)
                    did(V.tensor_tensor(carry[:, h4, :], a_first[:, h4, :], h0[:, h4, :], ALU.mult))
                    dve.wait_ge(lru_act, 2 * CH + half + 1)
                    did(V.tensor_tensor(u_g[:, h4, :], u_g[:, h4, :], i_g[:, h4, :], ALU.mult))
                    settle()
                    did(V.tensor_tensor(u_first[:, h4, :], u_first[:, h4, :], carry[:, h4, :], ALU.add))
                    did(V.memset(a_first[:, h4, :], 0.0))
                    did(V.memset(a_g[:, h4, 0:1], 0.0))
                    settle()
                    did(V.tensor_tensor_scan(r_h[:, h4, :].rearrange("p c t -> p (c t)"),
                                             a_g[:, h4, :].rearrange("p c t -> p (c t)"),
                                             u_g[:, h4, :].rearrange("p c t -> p (c t)"),
                                             0.0, ALU.mult, ALU.add))
                    if half == 0:
                        dve.wait_ge(evacuated[0], USE_Q)
                        dve.wait_ge(evacuated[1], USE_Q)
                    settle()
                    for c in range(4 * half, 4 * half + 4):
                        V.tensor_tensor(sq[:, c, :], r_h[:, c, :], gate[:, c, :],
                                        ALU.mult).then_inc(src_ready, 1)
                publish(PUB_OUT[0])
                V.tensor_copy(h_last[:, :, 0:1], r_h[:, :, TP - 1:TP]).then_inc(states_ready, 1)
                V.tensor_copy(h_last[:, :, 1:],
                              r_h[:, :, TP:T].rearrange("p c (s w) -> p c s w", s=NSEQ)[:, :, :, SL - 1]
                              ).then_inc(states_ready, 1)

            def conformer():
                for c in range(CH):
                    dve.wait_ge(slab_used, SLABS + IN0 + 2 * c + 2)
                    dve.wait_ge(evacuated[0], USES + USE_IN + c + 1)
                    b = col("cf_b_pw1", c)
                    V.scalar_tensor_tensor(out=z_ext[:, c, CF_W - 1:ZEXT_S], in0=ps[:, LIN + 1, 0:TP],
                                           scalar=b, in1=glu_gate[:, c % 2, 0:TP],
                                           op0=ALU.add, op1=ALU.mult).then_inc(glu_ready, 1)
                    V.scalar_tensor_tensor(
                        out=seqs(z_ext[:, c, ZEXT_S:ZEXT])[:, :, CF_W - 1:],
                        in0=seqs(ps[:, LIN + 1, TP:T]), scalar=b, in1=seqs(glu_gate[:, c % 2, TP:T]),
                        op0=ALU.add, op1=ALU.mult).then_inc(evacuated[1], 1)
                    settle()
                    dve.wait_ge(glu_ready, c + 1)
                    dve.wait_ge(evacuated[1], USES + USE_IN + c + 1)
                    wk = cols[:, COLS["cf_dw_w"]:COLS["cf_dw_w"] + CF_W * CH].rearrange(
                        "p (k c) -> p c k", c=CH)[:, c, :]
                    zs = z_ext[:, c, ZEXT_S:ZEXT]
                    for t in range(SL):
                        did(V.tensor_tensor(conv_prod[:, :, t, :], seqs(zs)[:, :, t:t + CF_W],
                                            wk.unsqueeze(1).to_broadcast([P, NSEQ, CF_W]), ALU.mult))
                    sums = [cv[:, c, 0:TP], cv_odd]
                    for k in range(SIDE_TAPS, CF_W):
                        src, w = z_ext[:, c, k:k + TP], col("cf_dw_w", k * CH + c)
                        dst = sums[(k - SIDE_TAPS) % 2]
                        if k == SIDE_TAPS:
                            did(V.tensor_scalar(dst, src, w, col("cf_dw_b", c), ALU.mult, ALU.add))
                        elif k == SIDE_TAPS + 1:
                            did(V.tensor_scalar(dst, src, w, None, ALU.mult))
                        else:
                            dve.wait_ge(step, steps[0] - 1)
                            did(V.scalar_tensor_tensor(out=dst, in0=src, scalar=w, in1=dst,
                                                       op0=ALU.mult, op1=ALU.add))
                        if k == CF_W // 2 + SIDE_TAPS // 2:
                            did(V.tensor_reduce(seqs(cv[:, c, TP:T]), conv_prod, AX_X, ALU.add))
                    settle()
                    did(V.tensor_tensor(sums[0], sums[0], sums[1], ALU.add))
                    did(V.tensor_scalar(cv[:, c, TP:T], cv[:, c, TP:T], col("cf_dw_b", c), None, ALU.add))
                    settle()
                    dve.wait_ge(taps_summed, (SIDE_TAPS - 1) * (c + 1))
                    if c == CH - 1:
                        dve.wait_ge(pool_sum_read, CH - 1)
                    V.tensor_tensor(sums[0], sums[0], cv_pool[:, c % 2, :], ALU.add).then_inc(
                        pool_sum_read if c < CH - 1 else src_ready, 1)
                dve.wait_ge(std_ready, SUM_MEAN + 1)
                dve.wait_ge(src_ready, SRC_CONV)
                V.tensor_tensor(cv, cv, mean.unsqueeze(1).to_broadcast([P, CH, T]),
                                ALU.subtract).then_inc(src_ready, 1)
                dve.wait_ge(src_ready, SRC_CENTRED)
                V.tensor_tensor(sq_cf[:, 4:8, :], cv[:, 4:8, :], cv[:, 4:8, :], ALU.mult).then_inc(sq_dve, 1)
                invert(SUM_VAR)
                V.tensor_tensor(cv, cv, rstd[:, :].unsqueeze(1).to_broadcast([P, CH, T]),
                                ALU.mult).then_inc(src_ready, 1)
                publish(PUB_OUT[1])

            def route(L):
                for u in range(4 * NT):
                    dve.wait_ge(scored, 4 * NT * L + u + 1)
                    tile, b = u // 4, u % 4
                    V.tensor_copy(scores[0:TT, tile, 512 * b:512 * b + 512],
                                  ps[0:TT, 2 + u % 6, :]).then_inc(scores_copied, 1)
                dve.wait_ge(scores_copied, 4 * NT * (L + 1))
                with dve.Fori(0, NT) as tile:
                    n = [0]
                    start = ROUTE_STEPS * (tile + NT * L)

                    def tile_did(ins):
                        n[0] += 1
                        ins.then_inc(route_step, 1)

                    def tile_settle():
                        dve.wait_ge(route_step, start + n[0])
                        hold(dve, n[0])

                    r = slice(0, TT)
                    V.tensor_copy(work[r, A:A + GROUPS * KEYS], scores[r, bass.ds(tile, 1), :].rearrange(
                        "p o k -> p (o k)")).then_inc(tile_staged, 1)
                    dve.wait_ge(tile_staged, tile + (NT * L + 1))
                    hold(dve)
                    for g in range(GROUPS):
                        ins = V.max(top_v[r, g, 0:8], s_tile[r, g, :])
                    tile_did(ins)
                    tile_settle()
                    for g in range(GROUPS):
                        V.match_replace(s_rest[r, g, :], top_v[r, g, 0:8], s_tile[r, g, :], LOWEST)
                        ins = V.max_index(top_i[r, g, 0:8], top_v[r, g, 0:8], s_tile[r, g, :])
                    tile_did(ins)
                    tile_settle()
                    for g in range(GROUPS):
                        ins = V.max(top_v[r, g, 8:16], s_rest[r, g, :])
                    tile_did(ins)
                    tile_settle()
                    for g in range(GROUPS):
                        V.max_index(top_i[r, g, 8:16], top_v[r, g, 8:16], s_rest[r, g, :])
                    tv = top_v[r].rearrange("p (h two) k -> p h two k", two=2)
                    tile_did(V.tensor_tensor(cand[r].rearrange("p h (a b) -> p h a b", a=TOPK),
                                        tv[:, :, 0, :].unsqueeze(3).to_broadcast([TT, HEADS, TOPK, TOPK]),
                                        tv[:, :, 1, :].unsqueeze(2).to_broadcast([TT, HEADS, TOPK, TOPK]),
                                        ALU.add))
                    tile_settle()
                    V.tensor_copy(top_f[r], top_i[r])
                    for h in range(HEADS):
                        ins = V.max(best[r, h, 0:8], cand[r, h, :])
                    tile_did(ins)
                    tile_settle()
                    for h in range(HEADS):
                        V.match_replace(cand_rest[r, h, :], best[r, h, 0:8], cand[r, h, :], LOWEST)
                        ins = V.max_index(pos[r, h, 0:8], best[r, h, 0:8], cand[r, h, :])
                    tile_did(ins)
                    tile_settle()
                    for h in range(HEADS):
                        ins = V.max(best[r, h, 8:16], cand_rest[r, h, :])
                    tile_did(ins)
                    tile_settle()
                    for h in range(HEADS):
                        V.max_index(pos[r, h, 8:16], best[r, h, 8:16], cand_rest[r, h, :])
                    pk = picks_tok[r, 2, bass.ds(tile, 1), :].rearrange("p o (h k) -> p (o h) k", h=HEADS)
                    tile_did(V.tensor_tensor(pk, best[r], best[r, :, 0:1].to_broadcast([TT, HEADS, TOPK]),
                                        ALU.subtract))
                    tile_settle()
                    posf = pos[r].rearrange("p h k -> p (h k)")
                    V.tensor_scalar(pos_ab[r, 0, :], posf, 4, None, ALU.logical_shift_right)
                    tile_did(V.tensor_scalar(pos_ab[r, 1, :], posf, 15, None, ALU.bitwise_and))
                    tile_settle()
                    tile_did(V.tensor_copy(pos_f[r], pos_ab[r]))
                    tile_settle()
                    for s in range(2):
                        pf = pos_f[r, s, :].rearrange("p (h k) -> p h k", h=HEADS)
                        tile_did(V.tensor_tensor(
                            hot[s][r], pf.unsqueeze(3).to_broadcast([TT, HEADS, TOPK, TOPK]),
                            iota[r, 0:TOPK].unsqueeze(1).unsqueeze(1).to_broadcast([TT, HEADS, TOPK, TOPK]),
                            ALU.is_equal))
                    tile_settle()
                    tf = top_f[r].rearrange("p (h two) k -> p h two k", two=2)
                    for s in range(2):
                        tile_did(V.tensor_tensor(
                            hot[s][r], hot[s][r],
                            tf[:, :, s, :].unsqueeze(2).to_broadcast([TT, HEADS, TOPK, TOPK]), ALU.mult))
                    tile_settle()
                    for s in range(2):
                        tile_did(V.tensor_reduce(
                            picks_tok[r, s, bass.ds(tile, 1), :].rearrange("p o k -> p (o k)"),
                            hot[s][r].rearrange("p h k a -> p (h k) a"), AX_X, ALU.add))
                    tile_settle()
                    assert n[0] == ROUTE_STEPS, n[0]
                gates = picks_tok[0:TT, 2, :, :].rearrange("p t (h k) -> p (t h) k", h=HEADS)
                dve.wait_ge(exp_ready, L + 1)
                did(V.tensor_reduce(head_sum[0:TT, :], gates, AX_X, ALU.add))
                settle()
                did(V.reciprocal(head_sum[0:TT, :], head_sum[0:TT, :]))
                settle()
                V.tensor_tensor(gates, gates, head_sum[0:TT, :].unsqueeze(2).to_broadcast(
                    [TT, NT * HEADS, TOPK]), ALU.mult).then_inc(picks_ready, 1)

            def expand_gates(half_index, half):
                first = GCH * half_index

                def onehots(g, buf):
                    if not (isinstance(g, int) and first + g < GBUF):
                        dve.wait_ge(expanded, g + (first + 1 - GBUF))
                    tok = bass.ds(g * GTOK, GTOK)
                    for out, keys_of, kind, n, ready in (
                            (mask_i, iota_rep[:, half * HT:(half + 1) * HT, :], 0, HT, masks_ready),
                            (onehot_j, iota_rep, 1, KEYS, js_ready)):
                        shape = [P, GTOK // 2, n, 2]
                        V.tensor_tensor(pairs(out[:, buf, :, :]), keys_of.unsqueeze(1).to_broadcast(shape),
                                        per_token(picks_b[:, kind, tok], shape),
                                        ALU.is_equal).then_inc(ready, 1)
                    dve.wait_ge(masks_ready, g + (first + 1))
                    V.tensor_tensor(pairs(onehot_i[1][:, buf, :, :]), pairs(mask_i[:, buf, :, :]),
                                    per_token(gate_terms[:, 1, tok], [P, GTOK // 2, HT, 2]),
                                    ALU.mult).then_inc(seconds_ready, 1)

                def apply(g, buf):
                    dve.wait_ge(expanded, g + (first + 1))
                    tok = hidden[:, :, bass.ds(g * GTOK, GTOK)]
                    V.tensor_tensor(tok, ps[:, GBANKS[buf], :].rearrange("p (t i) -> p i t", t=GTOK), tok,
                                    ALU.mult).then_inc(gated, 1)

                def round(q):
                    for b in range(GBUF):
                        onehots(GBUF * q + (b + 2), (b + 2) % GBUF)
                        apply(GBUF * q + b, b)

                onehots(0, 0)
                onehots(1, 1)
                round(0)
                with dve.Fori(1, GCH // GBUF - 1) as q:
                    round(q)
                for g in range(GCH - GBUF, GCH):
                    if g + 2 < GCH:
                        onehots(g + 2, (g + 2) % GBUF)
                    apply(g, g % GBUF)

            def gated_lo(tiles):
                with dve.Fori(0, HT // 4) as q:
                    for k in range(4):
                        dve.wait_ge(g_hi_ready, 4 * q + (tiles + k + 1))
                        V.tensor_tensor(g_lo[:, k, :], hidden_tile(4 * q + k),
                                        g_hi[:, k, :].bitcast(F32), ALU.subtract).then_inc(g_lo_ready, 1)

            def add_acc(n_slabs, c0):
                dve.wait_ge(slab_used, n_slabs)
                for c in range(4):
                    V.tensor_tensor(x[:, c0 + c, :], ps[:, ACC + c, 0:T], x[:, c0 + c, :],
                                    ALU.add).then_inc(x_updated, 1)

            def add_projection(L):
                for n in range(OUT_N):
                    dve.wait_ge(slab_used, L * SLABS + OUT0 + n + 1)
                    bias = 0.0 if L == 0 else col("cf_b_pw2", n)
                    V.scalar_tensor_tensor(out=x[:, n, :], in0=ps[:, LIN + n % 2, 0:T], scalar=bias,
                                           in1=x[:, n, :], op0=ALU.add, op1=ALU.add).then_inc(x_updated, 1)

            def peer(L):
                base = L * SLABS
                use = L * USES
                squares(L * X_VD + X_MIX)
                normed(SUM_FFN[L], "norm_ffn", L * CH)
                publish(PUB_FFN[L])
                route(L)
                dve.wait_ge(picks_copied, 3 * L + 3)
                for k in range(2):
                    did(V.tensor_copy(gate_terms[:, k, :], picks[:, 2, :]))
                    settle()
                    did(V.tensor_tensor(picks[:, 2, :], picks[:, 2, :], gate_terms[:, k, :], ALU.subtract))
                    settle()
                did(V.tensor_copy(picks_b, picks[:, 0:2, :]))
                did(V.tensor_copy(iota_rep, iota[:, :].unsqueeze(2).to_broadcast([P, KEYS, 2])))
                settle()
                for b in range(2):
                    dve.wait_ge(evacuated[b], use + USE_MIX)
                expand_gates(2 * L, 0)
                gated_lo(256 * L)
                add_acc(base + MIX0, 0)
                gated_lo(256 * L + 64)
                add_acc(base + VC0 - 2, 4)
                for b in range(2):
                    dve.wait_ge(evacuated[b], use + USES)
                expand_gates(2 * L + 1, 1)
                gated_lo(256 * L + 128)
                add_acc(base + VD0, 0)
                gated_lo(256 * L + 192)
                add_acc(base + SLABS, 4)

            squares(0)
            did(V.memset(ext[:, :, 0:RG_W - 1], 0.0))
            state = col("state_conv", 0, 192).rearrange("p (c s k) -> p c s k", c=CH, s=NSEQ)
            for c in range(CH):
                did(V.tensor_copy(seqs(ext[:, c, EXT_S:EXT])[:, :, 0:RG_W - 1], state[:, c, :, :]))
            decay_columns()
            normed(SUM_MIX[0], "norm_mix", 0)
            publish(PUB_MIX[0])
            settle()
            rg_mixer()
            add_projection(0)
            peer(0)
            squares(X_VD)
            did(V.memset(z_ext[:, :, 0:CF_W - 1], 0.0))
            dve.wait_ge(loaded_l, 16 * 7)
            for c in range(CH):
                did(V.tensor_copy(seqs(z_ext[:, c, ZEXT_S:ZEXT])[:, :, 0:CF_W - 1], cstate[:, c, :, :]))
            normed(SUM_MIX[1], "norm_mix", CH)
            publish(PUB_MIX[1])
            settle()
            conformer()
            add_projection(1)
            peer(1)
            squares(DEPTH * X_VD)
            normed(SUM_FINAL, "norm_final", 0)


def _columns(v):
    return v.reshape(-1, CH, P).transpose(2, 0, 1).reshape(P, -1)


def _linear_slabs(w):
    return w.reshape(CH, P, -1, P).transpose(2, 1, 0, 3).reshape(-1, P, D)


def _layer_slabs(np, w_in, order, w_out, w_q, u, v):
    w_in = _linear_slabs(w_in)[order]
    u = u.reshape(P, P, CH, P).transpose(0, 3, 2, 1).reshape(2, HT, P, D)
    v = v.reshape(2, HT // 2, 2, P, 2, 512).transpose(0, 4, 1, 3, 2, 5).reshape(2, 2, HT // 2, P, D)
    mix = np.concatenate([v[0, 1][:, None], u[1].reshape(HT // 2, 2, P, D)], axis=1).reshape(-1, P, D)
    return [w_in, _linear_slabs(w_out), _linear_slabs(w_q), u[0], v[0, 0], mix, v[1, 0], v[1, 1]]


def kernel(**inputs):
    import numpy as _np
    import concourse.bacc as _bacc
    from concourse import mybir as _mybir
    from concourse.bass_utils import run_bass_kernel_spmd as _run

    a = {k: _np.asarray(v) for k, v in inputs.items()}
    first = list(range(CH))
    gate_last = [CH + c for c in first] + first
    by_pairs = [n for c in first for n in (CH + c, c)]
    slabs = []
    slabs += _layer_slabs(_np, a["rg_w_in"][0], gate_last, a["rg_w_out"][0], a["peer_w_q"][0],
                          a["peer_u"][0], a["peer_v"][0])
    slabs += _layer_slabs(_np, a["cf_w_pw1"][0], by_pairs, a["cf_w_pw2"][0], a["peer_w_q"][1],
                          a["peer_u"][1], a["peer_v"][1])
    x0 = _np.concatenate([a["x_prompt"].reshape(TP, D), a["x_sample"].reshape(TS, D)], axis=0)
    packed = []
    for name in ("norm_mix", "norm_ffn", "norm_final", "rg_conv_w", "rg_conv_b", "rg_b_a", "rg_b_i",
                 "rg_lambda", "cf_b_pw1", "cf_dw_w", "cf_dw_b", "cf_ln_g", "cf_ln_b", "cf_b_pw2"):
        packed.append(_columns(a[name]))
    packed.append(a["state_rglru_h"].reshape(NSEQ, CH, P).transpose(2, 1, 0).reshape(P, -1))
    packed.append(a["state_rglru_conv"].reshape(NSEQ, RG_W - 1, CH, P).transpose(3, 2, 0, 1).reshape(P, -1))
    gates = _np.stack([a["rg_w_a"][0], a["rg_w_i"][0]])
    arrays = {
        "x": x0.reshape(T, CH, P).transpose(2, 1, 0),
        "stream": _np.concatenate(slabs, axis=0),
        "cols": _np.concatenate(packed, axis=1),
        "keys": a["peer_sub_keys"].reshape(DEPTH, GROUPS, KEYS, P).transpose(0, 3, 1, 2),
        "blocks": gates.reshape(2, CH, 2, 64, 64).transpose(0, 2, 3, 1, 4),
        "cstate": a["state_conformer_conv"].reshape(NSEQ, CF_W - 1, CH, P).transpose(3, 2, 0, 1),
    }
    arrays = {k: _np.ascontiguousarray(v) for k, v in arrays.items()}

    nc = _bacc.Bacc("TRN2", target_bir_lowering=False, num_devices=1)
    f32 = _mybir.dt.float32
    args = [nc.dram_tensor(f"{k}_dram", v.shape, f32, kind="ExternalInput").ap() for k, v in arrays.items()]
    outs = {"y_t": (P, CH, T), "h_t": (P, CH, 1 + NSEQ), "rgc_t": (P, CH, 1 + NSEQ, RG_W - 1),
            "cfp_t": (P, CH, CF_W - 1), "cfs_t": (P, CH, NSEQ, CF_W - 1)}
    args += [nc.dram_tensor(f"{k}_dram", v, f32, kind="ExternalOutput").ap() for k, v in outs.items()]
    build(nc, *args)
    r = _run(nc, [{f"{k}_dram": v for k, v in arrays.items()}], core_ids=[0]).results[0]

    y = r["y_t_dram"].transpose(2, 1, 0).reshape(T, D)
    h = r["h_t_dram"].transpose(2, 1, 0).reshape(1 + NSEQ, D)
    rgc = r["rgc_t_dram"].transpose(2, 3, 1, 0).reshape(1 + NSEQ, RG_W - 1, D)
    cfp = r["cfp_t_dram"].transpose(2, 1, 0).reshape(1, 1, CF_W - 1, D)
    cfs = r["cfs_t_dram"].transpose(2, 3, 1, 0).reshape(1, NSEQ, CF_W - 1, D)
    return (y[:TP].reshape(1, TP, D), y[TP:].reshape(NSEQ, SL, D), h[None, :1], rgc[None, :1], cfp,
            h[None, 1:], rgc[None, 1:], cfs)
```
